# Optimizing a Trainium2 kernel written in Bass

```python
import jax, jax.numpy as jnp
from jax import lax
import numpy as np

D_MODEL = 1024
BATCH = 1
SEQ = 256
DEPTH = 2

CHUNK = 64
D_MIX = 1024
GROUP_W = 256
HEAD_DIM = 64
A_Q_HEADS = 4
A_KV_HEADS = 2
A_WINDOW = 128
A_BACK = A_WINDOW // CHUNK - 1
POOL_WINDOWS = (2, 4, 8, 16)
POOL_CH = GROUP_W // len(POOL_WINDOWS)
C_HEADS = 4
C_BACK = 8
REL_CLIP = 128
RG_BLOCKS = 4
RG_BS = GROUP_W // RG_BLOCKS
CONV_W = 4
RG_C = 8.0
D_FF = 3584
N_EXPERTS = 8
TOP_K = 2
MOE_BLOCK = 256
N_DENSE = (DEPTH + 1) // 2
N_MOE = DEPTH // 2
EPS = 1e-6
NEG_INF = -1e30
IN_SPLITS = (A_Q_HEADS * HEAD_DIM, A_KV_HEADS * HEAD_DIM, A_KV_HEADS * HEAD_DIM,
             GROUP_W,
             C_HEADS * HEAD_DIM, C_HEADS * HEAD_DIM, C_HEADS * HEAD_DIM,
             GROUP_W, GROUP_W)
D_IN = 2048

kernel_name = 'hybrid_streaming_head_group_block'

def rms_norm(x, g):
    x32 = x.astype(jnp.float32)
    y = x32 * lax.rsqrt(jnp.mean(x32 * x32, axis=-1, keepdims=True) + EPS)
    return (y * g.astype(jnp.float32)).astype(x.dtype)

def gather_chunk_band(t, n_back):
    b, s, h, d = t.shape
    nc = s // CHUNK
    tc = t.reshape(b, nc, CHUNK, h, d)
    tp = jnp.pad(tc, ((0, 0), (n_back, 0), (0, 0), (0, 0), (0, 0)))
    return jnp.concatenate([tp[:, j:j + nc] for j in range(n_back + 1)], axis=2)

def band_valid(nc, n_back):
    src_chunk = jnp.arange(nc)[:, None] - n_back + jnp.arange(n_back + 1)[None, :]
    return jnp.repeat(src_chunk >= 0, CHUNK, axis=1)

def sliding_window_sink_attention(q, k, v, sinks):
    b, s, _ = q.shape
    nc = s // CHUNK
    g = A_Q_HEADS // A_KV_HEADS
    qh = q.reshape(b, nc, CHUNK, A_KV_HEADS, g, HEAD_DIM)
    kb = gather_chunk_band(k.reshape(b, s, A_KV_HEADS, HEAD_DIM), A_BACK)
    vb = gather_chunk_band(v.reshape(b, s, A_KV_HEADS, HEAD_DIM), A_BACK)
    scores = jnp.einsum('bcqkgd,bcjkd->bckgqj', qh, kb).astype(jnp.float32) * (HEAD_DIM ** -0.5)
    valid = band_valid(nc, A_BACK)[None, :, None, None, None, :]
    scores = jnp.where(valid, scores, NEG_INF)
    sink = jnp.broadcast_to(
        sinks.astype(jnp.float32).reshape(A_KV_HEADS, g)[None, None, :, :, None, None],
        scores.shape[:-1] + (1,))
    probs = jax.nn.softmax(jnp.concatenate([scores, sink], axis=-1), axis=-1)[..., :-1]
    out = jnp.einsum('bckgqj,bcjkd->bcqkgd', probs.astype(v.dtype), vb)
    return out.reshape(b, s, A_Q_HEADS * HEAD_DIM)

def multiscale_pool(p, pool_w, pool_scale):
    b, s, _ = p.shape
    p32 = p.astype(jnp.float32)
    csp = jnp.pad(jnp.cumsum(p32, axis=1), ((0, 0), (1, 0), (0, 0)))
    pos = jnp.arange(1, s + 1, dtype=jnp.float32)[None, :, None]
    outs = []
    for gi, w in enumerate(POOL_WINDOWS):
        cg = csp[:, :, gi * POOL_CH:(gi + 1) * POOL_CH]
        lagged = jnp.pad(cg, ((0, 0), (w - 1, 0), (0, 0)))[:, :s]
        mean = (cg[:, 1:] - lagged) / jnp.minimum(pos, float(w))
        outs.append(mean - p32[:, :, gi * POOL_CH:(gi + 1) * POOL_CH])
    d = jnp.stack(outs, axis=2).astype(p.dtype)
    y = jnp.einsum('bsgc,gce->bsge', d, pool_w).reshape(b, s, GROUP_W)
    return y * pool_scale

def chunk_relbias_attention(q, k, v, rel_bias):
    b, s, _ = q.shape
    nc = s // CHUNK
    band = (C_BACK + 1) * CHUNK
    qh = q.reshape(b, nc, CHUNK, C_HEADS, HEAD_DIM)
    kb = gather_chunk_band(k.reshape(b, s, C_HEADS, HEAD_DIM), C_BACK)
    vb = gather_chunk_band(v.reshape(b, s, C_HEADS, HEAD_DIM), C_BACK)
    rel = C_BACK * CHUNK + jnp.arange(CHUNK)[:, None] - jnp.arange(band)[None, :]
    idx = jnp.clip(rel, -REL_CLIP, REL_CLIP) + REL_CLIP
    bias = rel_bias.astype(jnp.float32)[:, idx]
    scores = jnp.einsum('bcqhd,bcjhd->bchqj', qh, kb).astype(jnp.float32) * (HEAD_DIM ** -0.5)
    scores = scores + bias[None, None]
    valid = band_valid(nc, C_BACK)[None, :, None, None, :]
    probs = jax.nn.softmax(jnp.where(valid, scores, NEG_INF), axis=-1)
    out = jnp.einsum('bchqj,bcjhd->bcqhd', probs.astype(v.dtype), vb)
    return out.reshape(b, s, C_HEADS * HEAD_DIM)

def causal_dwconv(x, w, bias):
    s = x.shape[1]
    xp = jnp.pad(x, ((0, 0), (CONV_W - 1, 0), (0, 0)))
    y = xp[:, 0:s] * w[0]
    for j in range(1, CONV_W):
        y = y + xp[:, j:j + s] * w[j]
    return y + bias

def block_diag_linear(x, w, bias):
    b, s, _ = x.shape
    y = jnp.einsum('bsnc,ncd->bsnd', x.reshape(b, s, RG_BLOCKS, RG_BS), w)
    return y.reshape(b, s, RG_BLOCKS * RG_BS) + bias

def scan_combine(c1, c2):
    a1, b1 = c1
    a2, b2 = c2
    return a1 * a2, a2 * b1 + b2

def rglru_branch(xd, gd, conv_w, conv_b, w_a, b_a, w_x, b_x, lam):
    xc = causal_dwconv(xd, conv_w, conv_b)
    r = jax.nn.sigmoid(block_diag_linear(xc, w_a, b_a)).astype(jnp.float32)
    i = jax.nn.sigmoid(block_diag_linear(xc, w_x, b_x))
    log_a = -RG_C * r * jax.nn.softplus(-lam.astype(jnp.float32))
    a = jnp.exp(log_a)
    mult = jnp.sqrt(-jnp.expm1(2.0 * log_a))
    bterm = mult * (i * xc).astype(jnp.float32)
    _, h = lax.associative_scan(scan_combine, (a, bterm), axis=1)
    return h.astype(xd.dtype) * jax.nn.gelu(gd)

def swiglu(h, w_gate, w_up, w_down):
    return (jax.nn.silu(h @ w_gate) * (h @ w_up)) @ w_down

def moe_swiglu(h, router_w, w_gate, w_up, w_down):
    b, s, d = h.shape
    x = h.reshape(-1, d)
    n = x.shape[0]
    logits = x.astype(jnp.float32) @ router_w.astype(jnp.float32)
    top_val, top_idx = lax.top_k(logits, TOP_K)
    gates = jax.nn.softmax(top_val, axis=-1)
    flat_e = top_idx.reshape(-1)
    flat_tok = jnp.repeat(jnp.arange(n), TOP_K)
    flat_g = gates.reshape(-1)
    order = jnp.argsort(flat_e)
    se, stok, sg = flat_e[order], flat_tok[order], flat_g[order]
    counts = jnp.bincount(flat_e, length=N_EXPERTS)
    starts = jnp.cumsum(counts) - counts
    padded = ((counts + MOE_BLOCK - 1) // MOE_BLOCK) * MOE_BLOCK
    pend = jnp.cumsum(padded)
    pstarts = pend - padded
    dest = pstarts[se] + (jnp.arange(n * TOP_K) - starts[se])
    n_blocks = -(-(n * TOP_K) // MOE_BLOCK) + N_EXPERTS
    xbuf = jnp.zeros((n_blocks * MOE_BLOCK, d), x.dtype).at[dest].set(x[stok])
    block_e = jnp.minimum(
        jnp.searchsorted(pend, jnp.arange(n_blocks) * MOE_BLOCK, side='right'), N_EXPERTS - 1)

    def expert_block(args):
        xb, e = args
        return swiglu(xb, w_gate[e], w_up[e], w_down[e])

    ybuf = lax.map(expert_block, (xbuf.reshape(n_blocks, MOE_BLOCK, d), block_e))
    y_slots = ybuf.reshape(-1, d)[dest] * sg[:, None].astype(x.dtype)
    out = jnp.zeros_like(x).at[stok].add(y_slots)
    return out.reshape(b, s, d)

def setup_inputs(seed: int = 0) -> dict:
    key = jax.random.key(seed)
    ks = jax.random.split(key, 32)
    f32 = jnp.float32
    nrm = lambda k, shape, sc: jax.random.normal(k, shape, f32) * sc
    u = jax.random.uniform(ks[16], (DEPTH, GROUP_W), f32, minval=0.9, maxval=0.999)
    sbase = u ** (1.0 / RG_C)
    rg_lambda = jnp.log(sbase) - jnp.log1p(-sbase)
    return {
        'x': nrm(ks[0], (BATCH, SEQ, D_MODEL), 1.0),
        'norm_mix_pre': 1.0 + nrm(ks[1], (DEPTH, D_MODEL), 0.05),
        'w_in': nrm(ks[2], (DEPTH, D_MODEL, D_IN), D_MODEL ** -0.5),
        'attn_sinks': nrm(ks[3], (DEPTH, A_Q_HEADS), 0.5),
        'pool_w': nrm(ks[4], (DEPTH, len(POOL_WINDOWS), POOL_CH, POOL_CH), POOL_CH ** -0.5),
        'pool_scale': 1.0 + nrm(ks[5], (DEPTH, GROUP_W), 0.1),
        'rel_bias': nrm(ks[6], (DEPTH, C_HEADS, 2 * REL_CLIP + 1), 0.1),
        'conv_w': nrm(ks[7], (DEPTH, CONV_W, GROUP_W), CONV_W ** -0.5),
        'conv_b': nrm(ks[8], (DEPTH, GROUP_W), 0.01),
        'rg_w_a': nrm(ks[9], (DEPTH, RG_BLOCKS, RG_BS, RG_BS), RG_BS ** -0.5),
        'rg_b_a': nrm(ks[10], (DEPTH, GROUP_W), 0.01),
        'rg_w_x': nrm(ks[11], (DEPTH, RG_BLOCKS, RG_BS, RG_BS), RG_BS ** -0.5),
        'rg_b_x': nrm(ks[12], (DEPTH, GROUP_W), 0.01),
        'rg_lambda': rg_lambda,
        'w_out': nrm(ks[13], (DEPTH, D_MIX, D_MODEL), D_MIX ** -0.5),
        'norm_mix_post': 1.0 + nrm(ks[14], (DEPTH, D_MODEL), 0.05),
        'norm_ffn_pre': 1.0 + nrm(ks[15], (DEPTH, D_MODEL), 0.05),
        'norm_ffn_post': 1.0 + nrm(ks[17], (DEPTH, D_MODEL), 0.05),
        'ffn_w_gate': nrm(ks[18], (N_DENSE, D_MODEL, D_FF), D_MODEL ** -0.5),
        'ffn_w_up': nrm(ks[19], (N_DENSE, D_MODEL, D_FF), D_MODEL ** -0.5),
        'ffn_w_down': nrm(ks[20], (N_DENSE, D_FF, D_MODEL), D_FF ** -0.5),
        'router_w': nrm(ks[21], (N_MOE, D_MODEL, N_EXPERTS), D_MODEL ** -0.5),
        'moe_w_gate': nrm(ks[22], (N_MOE, N_EXPERTS, D_MODEL, D_FF), D_MODEL ** -0.5),
        'moe_w_up': nrm(ks[23], (N_MOE, N_EXPERTS, D_MODEL, D_FF), D_MODEL ** -0.5),
        'moe_w_down': nrm(ks[24], (N_MOE, N_EXPERTS, D_FF, D_MODEL), D_FF ** -0.5),
    }

def reference(x, norm_mix_pre, w_in, attn_sinks, pool_w, pool_scale, rel_bias, conv_w, conv_b,
              rg_w_a, rg_b_a, rg_w_x, rg_b_x, rg_lambda, w_out, norm_mix_post, norm_ffn_pre,
              norm_ffn_post, ffn_w_gate, ffn_w_up, ffn_w_down, router_w, moe_w_gate, moe_w_up,
              moe_w_down):
    split_at = [int(v) for v in np.cumsum(IN_SPLITS)[:-1]]
    for l in range(DEPTH):
        h = rms_norm(x, norm_mix_pre[l])
        z = h @ w_in[l]
        qa, ka, va, pin, qc, kc, vc, xd, gd = jnp.split(z, split_at, axis=-1)
        ya = sliding_window_sink_attention(qa, ka, va, attn_sinks[l])
        yb = multiscale_pool(pin, pool_w[l], pool_scale[l])
        yc = chunk_relbias_attention(qc, kc, vc, rel_bias[l])
        yd = rglru_branch(xd, gd, conv_w[l], conv_b[l], rg_w_a[l], rg_b_a[l],
                          rg_w_x[l], rg_b_x[l], rg_lambda[l])
        y = jnp.concatenate([ya, yb, yc, yd], axis=-1) @ w_out[l]
        x = x + rms_norm(y, norm_mix_post[l])
        h = rms_norm(x, norm_ffn_pre[l])
        if l % 2 == 0:
            f = swiglu(h, ffn_w_gate[l // 2], ffn_w_up[l // 2], ffn_w_down[l // 2])
        else:
            f = moe_swiglu(h, router_w[l // 2], moe_w_gate[l // 2], moe_w_up[l // 2],
                           moe_w_down[l // 2])
        x = x + rms_norm(f, norm_ffn_post[l])
    return x


_drawn_inputs = setup_inputs


def setup_inputs(seed=0):
    import zlib

    import numpy as np

    out = dict(_drawn_inputs(seed))
    spreads = {}
    factors = {'attn_sinks': 8.0, 'rg_b_a': 2.991, 'rg_b_x': 8.0}
    for name, (base, spread) in spreads.items():
        noise = np.random.default_rng([zlib.crc32(name.encode()), seed]).standard_normal(out[name].shape)
        drawn = base * np.exp(spread * noise) if base else spread * noise
        out[name] = __import__('jax').numpy.asarray(drawn.astype(out[name].dtype))
    for name, factor in factors.items():
        out[name] = (out[name] * factor).astype(out[name].dtype)
    return out
```

```python
import concourse.bass as bass
from concourse import mybir

F32 = mybir.dt.float32
F32R = mybir.dt.float32r
I32 = mybir.dt.int32
ALU = mybir.AluOpType
ACT = mybir.ActivationFunctionType
AX = mybir.AxisListType

P = 128
S = 256
TT = S // P
D = 1024
KT = D // P
FF = 3584
FB = FF // 512
NE = 8
HD = 64
EPS = 1e-6
NEG = -1e30
RELCLIP = 128
RELW = 384
UNIT = 2048
NRING = 7
NHI = 6
LEAD = 5
MOE_UNITS = 6 * FB
MAX_EXTRA = 3
NO_SLOT = 1000.0
WIN_ORDER = [6, 7, 2, 0, 1, 3, 4, 5]
WOUT_ORDER = [1, 3, 0, 2]
V_MIXPRE, V_FFNPRE, V_PSCALE, V_CONVB, V_BA, V_BX, V_LAM, V_CONVW, V_ROWS = 0, 16, 32, 36, 40, 44, 48, 52, 68


def ffn_units():
    out = []
    for j in range(FB + 1):
        if j < FB:
            out += [("gate", j, 0), ("gate", j, 1), ("up", j, 0), ("up", j, 1)]
        if j > 0:
            out += [("down", j - 1, 0), ("down", j - 1, 1)]
    return out


FFN_UNITS = ffn_units()
FFN_AT = {u: n for n, u in enumerate(FFN_UNITS)}
MIX_UNITS = [("win", c, 0) for c in WIN_ORDER] + [("wout", r, 0) for r in WOUT_ORDER]
STATIC = [(0, u) for u in MIX_UNITS + FFN_UNITS] + [(1, u) for u in MIX_UNITS]
NSTATIC = len(STATIC)
LAYER_AT = [0, len(MIX_UNITS) + MOE_UNITS]
FFN0_AT = len(MIX_UNITS)


def loads(u, slot):
    return sum(4 if STATIC[n][1] == ("win", 0, 0) else 1 for n in range(u + 1) if n % NRING == slot)


def moe_slot(m):
    order = [(NSTATIC + s) % NRING for s in range(3)] + list(range(NRING, 2 * NRING))
    order += [(NSTATIC + s) % NRING for s in range(3, NRING)]
    return order[m % (2 * NRING)]


def build(nc, A, out):
    base = -(-nc.sbuf_base // 64) * 64
    place = [base]

    def sb(name, shape, dt=F32, at=None):
        size = 4
        for n in shape[1:]:
            size *= n
        off = place[0] if at is None else at
        if at is None:
            place[0] += -(-size // 32) * 32
        return nc.alloc_sbuf_tensor_at(name, shape, dt, offset=off)

    ring_a = sb("ring_a", [P, NRING, UNIT])
    ring_a_lo = sb("ring_a_lo", [P, NRING, UNIT], F32R, at=base)
    mix_base = place[0]
    ring_b = sb("ring_b", [P, NRING, UNIT])
    ring_b_lo = sb("ring_b_lo", [P, NRING, UNIT], F32R, at=mix_base)
    mix_end = place[0]
    w_hi = sb("w_hi", [P, NHI, UNIT], F32R)
    x_at = place[0]
    x = sb("x", [P, TT, D])
    hhi_at = place[0]
    h_hi = sb("h_hi", [P, KT * S], F32R)
    hlo_at = place[0]
    h_lo = sb("h_lo", [P, KT * S], F32R)
    xn_at = place[0]
    xn = sb("xn", [P, TT, D])
    gpost_at = place[0]
    gpost = sb("gpost", [P, D])
    s_buf = sb("s_buf", [P, 512])
    t_buf = sb("t_buf", [P, 512])
    gpre_at = place[0]
    place[0] += 1024
    pick = sb("pick", [P, TT, P])
    pickg = sb("pickg", [P, TT, P])
    put = sb("put", [P, TT, P])
    gpre = sb("gpre", [P, D], at=gpre_at)
    vrows = sb("vrows", [V_ROWS, P], at=gpost_at)
    vec = sb("vec", [P, V_ROWS])
    ident = sb("ident", [P, P])
    iota_row = sb("iota_row", [P, P])
    rw = sb("rw", [P, KT, NE])
    rw_hi = sb("rw_hi", [P, KT * NE], F32R)
    rw_lo = sb("rw_lo", [P, KT * NE], F32R)
    small = sb("small", [P, 64])
    rt = sb("rt", [P, 320])
    ev = sb("ev", [1, 8], I32)
    assert place[0] <= nc.sbuf_usable_end, place[0]
    end = place[0]

    place[0] = mix_base
    hankel = sb("hankel", [P, 8, S])
    mask_a1 = sb("mask_a1", [P, S])
    mask_c1 = sb("mask_c1", [P, S])
    mask_t0 = sb("mask_t0", [P, P])
    chunk_l = sb("chunk_l", [P, P])
    flip = sb("flip", [P, P])
    invw = sb("invw", [P, 2, S])
    pool_w = sb("pool_w_sb", [P, 2, 2, HD])
    rg_wa = sb("rg_wa", [P, 2, 2, HD])
    rg_wx = sb("rg_wx", [P, 2, 2, HD])
    ffn_at = place[0]
    q_a = sb("q_a", [P, 2, S])
    k_a = sb("k_a", [P, S])
    v_a = sb("v_a", [P, TT, P])
    q_c = sb("q_c", [P, 2, S])
    k_c = sb("k_c", [P, 2, S])
    v_c = sb("v_c", [P, TT, S])
    xd = sb("xd", [P, 2, S + 4])
    gd = sb("gd", [P, 2, S])
    pin = sb("pin", [P, 2, S + 16])
    win_a = sb("win_a", [P, 2, S + 16])
    win_b = sb("win_b", [P, 2, S + 16])
    pd = sb("pd", [P, 2, S])
    xc = sb("xc", [P, 2, S])
    gr = sb("gr", [P, 2, S])
    gi = sb("gi", [P, 2, S])
    th = sb("th", [P, 2, S])
    aa = sb("aa", [P, 2, S])
    probs_t = sb("probs_t", [P, 3, 512])
    assert place[0] <= mix_end, (place[0], mix_end)
    probs = sb("probs", [P, 3, 512], at=xn_at)
    relrow = sb("relrow", [8, RELW], at=gpost_at + 1024)
    sil = sb("sil", [P, 4, S], at=ffn_at)
    hid = sb("hid", [P, 4, S], at=ffn_at + 4096)
    hid_hi = sb("hid_hi", [P, 4, S], F32R, at=ffn_at + 8192)
    hid_lo = sb("hid_lo", [P, 4, S], F32R, at=ffn_at + 12288)
    xg_hi, xg_lo = h_hi[:, 0:KT * P], h_lo[:, 0:KT * P]
    mh_hi, mh_lo = h_hi[:, KT * P:KT * P + 512], h_lo[:, KT * P:KT * P + 512]
    glast = [sb("glast0", [P, 512], at=hhi_at + 6144), sb("glast1", [P, 512], at=hlo_at + 6144)]
    y_slots = sb("y_slots", [P, D], at=gpost_at)
    tri = sb("tri", [P, P], at=gpost_at)
    ones = sb("ones", [P, P], at=gpost_at + 512)
    iota_e = rt[:, 288:296]
    desc_e = rt[:, 296:304]
    xr = sb("xr", [P, TT, D], at=xn_at)

    bank = [nc.alloc_psum_tensor(f"bank{i}", [P, 512], F32) for i in range(8)]
    x_park = nc.dram_tensor("x_park", (P, TT, D), F32, kind="Internal").ap()
    rel_pad = nc.dram_tensor("rel_pad", (8, RELW), F32, kind="Internal").ap()

    names = {}

    def sem(name):
        names[name] = nc.alloc_semaphore(name)
        return names[name]

    slot_in = [sem(f"slot_in{i}") for i in range(2 * NRING)]
    x_in = [sem("x_in0"), sem("x_in1")]
    vrows_in = sem("vrows_in")
    params_in = sem("params_in")
    rel_in = sem("rel_in")
    rel_out = sem("rel_out")
    hankel_in = sem("hankel_in")
    gpost_in = sem("gpost_in")
    park_out = sem("park_out")
    xr_in = sem("xr_in")
    glast_in = sem("glast_in")
    out_done = sem("out_done")
    hi_done = sem("hi_done")
    lo_done = sem("lo_done")
    unit_used = sem("unit_used")
    rw_hi_done = sem("rw_hi_done")
    rw_lo_done = sem("rw_lo_done")
    gpre_in = sem("gpre_in")
    y_ps = sem("y_ps")
    consts = sem("consts")
    pool_step = sem("pool_step")
    act_step = sem("act_step")
    dve_step = sem("dve_step")
    vec_ps = sem("vec_ps")
    vec_done = sem("vec_done")
    lam_abs = sem("lam_abs")
    lam_exp = sem("lam_exp")
    lam_done = sem("lam_done")
    rel_row = sem("rel_row")
    ssq = sem("ssq")
    ms = sem("ms")
    root = sem("root")
    xn_done = sem("xn_done")
    ht_ps = sem("ht_ps")
    ht_hi = sem("ht_hi")
    ht_lo = sem("ht_lo")
    z_out = sem("z_out")
    pads = sem("pads")
    conv_done = sem("conv_done")
    gates_ps = sem("gates_ps")
    gates_done = sem("gates_done")
    decay_done = sem("decay_done")
    m2_done = sem("m2_done")
    mult_done = sem("mult_done")
    pool_ready = sem("pool_ready")
    pool_ps = sem("pool_ps")
    yb_done = sem("yb_done")
    yd_done = sem("yd_done")
    pe_pair = sem("pe_pair")
    sc_ps = {k: sem(f"sc_ps_{k}") for k in "ac"}
    nmax = {k: sem(f"nmax_{k}") for k in "ac"}
    exp_done = {k: sem(f"exp_{k}") for k in "ac"}
    sink_done = sem("sink_done")
    prob_done = {k: sem(f"prob_{k}") for k in "ac"}
    pt_ps = {k: sem(f"pt_ps_{k}") for k in "ac"}
    pt_out = {k: sem(f"pt_out_{k}") for k in "ac"}
    pv_ps = {k: sem(f"pv_ps_{k}") for k in "ac"}
    y_hi = {k: sem(f"y_hi_{k}") for k in "ac"}
    y_lo = {k: sem(f"y_lo_{k}") for k in "ac"}
    post_ssq = sem("post_ssq")
    post_ms = sem("post_ms")
    post_root = sem("post_root")
    x_done = sem("x_done")
    silu_done = sem("silu_done")
    h_done = sem("h_done")
    t_done = sem("t_done")
    hid_hi_done = sem("hid_hi_done")
    hid_lo_done = sem("hid_lo_done")
    logit_ps = sem("logit_ps")
    gate_arg = sem("gate_arg")
    gate_exp = sem("gate_exp")
    taken = sem("taken")
    rank_ps = sem("rank_ps")
    tables = sem("tables")
    acc_zero = sem("acc_zero")
    y_zero = sem("y_zero")
    y_evac = sem("y_evac")
    p_done = sem("p_done")
    pg_done = sem("pg_done")
    gather_ps = sem("gather_ps")
    xg_hi_done = sem("xg_hi_done")
    xg_lo_done = sem("xg_lo_done")
    put_ps = sem("put_ps")
    put_done = sem("put_done")
    scatter_ps = sem("scatter_ps")
    acc_added = sem("acc_added")

    def slot_ap(s):
        return ring_a[:, s, :] if s < NRING else ring_b[:, s - NRING, :]

    def unit_src(l, unit, e=None):
        kind, a, b = unit
        if kind == "win":
            return A["w_in"][l, :, 256 * a:256 * a + 256].rearrange("(k p) c -> p k c", p=P)
        if kind == "wout":
            return A["w_out"][l, 256 * a:256 * a + 256, :].rearrange("(k p) c -> p k c", p=P)
        if e is None:
            gate, up, down = A["ffn_w_gate"][0], A["ffn_w_up"][0], A["ffn_w_down"][0]
        else:
            gate, up, down = (A[f"moe_w_{n}"][0, bass.ds(e, 1)].rearrange("o a b -> (o a) b")
                              for n in ("gate", "up", "down"))
        if kind == "down":
            return down[512 * a + 256 * b:512 * a + 256 * b + 256, :].rearrange("(k p) c -> p k c", p=P)
        w = gate if kind == "gate" else up
        return w[512 * b:512 * b + 512, 512 * a:512 * a + 512].rearrange("(k p) c -> p k c", p=P)

    def unit_dst(s, unit):
        cols = {"win": 256, "wout": 1024, "down": 1024}.get(unit[0], 512)
        return slot_ap(s).rearrange("p (k c) -> p k c", c=cols)

    def load_unit(eng, s, l, unit, e=None):
        src, dst = unit_src(l, unit, e), unit_dst(s, unit)
        if unit == ("win", 0, 0):
            src = src.rearrange("p k (g b d) -> p k b g d", g=2, b=2)
            dst = dst.rearrange("p k (b g d) -> p k b g d", g=2, b=2)
            for b in range(2):
                for g in range(2):
                    eng.dma_start(dst[:, :, b, g], src[:, :, b, g]).then_inc(slot_in[s], 16)
        else:
            eng.dma_start(dst, src).then_inc(slot_in[s], 16)

    def ring_lo(s):
        return ring_a_lo[:, s, :] if s < NRING else ring_b_lo[:, s - NRING, :]

    def part(b):
        return b[:, :].rearrange("p (k s) -> p k s", k=4)

    def h_part(h, q):
        return h[:, :].rearrange("p (k s) -> p k s", k=KT)[:, 4 * (q % 2):4 * (q % 2) + 4, P * (q // 2):P * (q // 2) + P]

    def score_at(kind, t, h):
        if t == 0:
            return 0, h * P, h
        pair, n = (h // 2, h % 2) if kind == "a" else (h % 2, h // 2)
        return 1 + pair, n * S, 4 + 2 * pair + n

    ev_range = dict(min_val=0, max_val=NE - 1)

    def load_passes(eng):
        eng.wait_ge(tables, 1)
        return eng.value_load(ev[0:1, 0:1], min_val=NE, max_val=NE + MAX_EXTRA)

    def load_last(eng):
        return eng.value_load(ev[0:1, 4:5], min_val=NE - 1, max_val=NE + MAX_EXTRA - 1)

    block = nc.Block()
    block.__enter__()

    @block.sync
    def _(sp):
        for t in range(TT):
            sp.dma_start(x[:, t, :], A["x"][0, t * P:t * P + P, :]).then_inc(x_in[t], 16)
        sp.dma_start(gpre[:, :], A["norm_mix_pre"][0].partition_broadcast(P)).then_inc(gpre_in, 16)
        for n, (l, unit) in enumerate(STATIC):
            if n >= NRING:
                sp.wait_ge(unit_used, n - NRING + 1)
            load_unit(sp, n % NRING, l, unit)

        def expert(i, e, first):
            for m, unit in enumerate(FFN_UNITS):
                s = moe_slot(m)
                if first and m < 2 * NRING:
                    if s < NRING:
                        last = max(n for n in range(NSTATIC) if n % NRING == s)
                        sp.wait_ge(unit_used, last + 1)
                    else:
                        sp.wait_ge(y_lo["c"], 2)
                        sp.wait_ge(yd_done, 2)
                        sp.wait_ge(yb_done, 2)
                else:
                    sp.wait_ge(unit_used, NSTATIC + MOE_UNITS * i + m - 2 * NRING + 1)
                load_unit(sp, s, 1, unit, e)

        expert(0, 0, True)
        with sp.Fori(1, NE) as i:
            expert(i, i, False)
        n_pass = load_passes(sp)
        with sp.If(n_pass > NE):
            with sp.Fori(NE, n_pass) as i:
                e = sp.value_load(ev[0:1, bass.ds(i - (NE - 1), 1)], **ev_range)
                expert(i, e, False)
        for t in range(TT):
            sp.wait_ge(x_done, 14 + 2 * t)
            sp.dma_start(out[0, t * P:t * P + P, :], x[:, t, :]).then_inc(out_done, 16)
        sp.wait_ge(out_done, 32)

    @block.gpsimd
    def _(gp):
        steps = [0]

        def step(ins):
            steps[0] += 1
            ins.then_inc(pool_step, 1)
            gp.wait_ge(pool_step, steps[0])

        def diag(t, value, mult, pattern):
            step(gp.memset(t[:, :], 0.0))
            step(gp.affine_select(out=t[:, :], in_=t[:, :], compare_op=ALU.not_equal, fill=1.0, base=value,
                                  pattern=pattern, channel_multiplier=mult))

        diag(ident, 0, 1, [[-1, P]])
        gp.engine_nop().then_inc(consts, 1)
        gp.dma_start(relrow[:, 0:2 * RELCLIP + 1], A["rel_bias"].rearrange("l h r -> (l h) r")).then_inc(rel_in, 16)
        for src, dst in ((A["pool_w"], pool_w), (A["rg_w_a"], rg_wa), (A["rg_w_x"], rg_wx)):
            v = src.rearrange("l (h a) c e -> a c l h e", a=2)
            for a in range(2):
                gp.dma_start(dst[HD * a:HD * a + HD, :, :, :], v[a]).then_inc(params_in, 16)
        gp.dma_start(rw[:, :, :], A["router_w"].rearrange("o (k p) e -> p (o k) e", p=P)).then_inc(params_in, 16)
        gp.dma_start(small[:, 0:8], A["attn_sinks"].rearrange("l h -> (l h)").partition_broadcast(P)).then_inc(params_in, 16)
        gp.wait_ge(rel_row, 1)
        gp.dma_start(rel_pad, relrow[:, :]).then_inc(rel_out, 16)
        diag(flip, -(P - 1), 1, [[1, P]])
        step(gp.memset(chunk_l[:, :], 0.0))
        for t in (mask_a1, mask_c1, mask_t0):
            step(gp.memset(t[:, :], 0.0))
        for r in (0, 64):
            step(gp.memset(chunk_l[r:r + 1, 0:64], 1.0))
            step(gp.memset(chunk_l[r + 32:r + 33, 64:128], 1.0))
            step(gp.memset(mask_t0[r:r + 1, 64:128], NEG))
            step(gp.memset(mask_a1[r:r + 1, 0:64], NEG))
            step(gp.memset(mask_a1[r:r + 1, 192:256], NEG))
            step(gp.memset(mask_a1[r + 32:r + 33, 0:128], NEG))
            step(gp.memset(mask_c1[r:r + 1, 192:256], NEG))
        step(gp.iota(iota_row[:, :], pattern=[[1, P]], base=0, channel_multiplier=0,
                     allow_small_or_imprecise_dtypes=True))
        step(gp.iota(iota_e, pattern=[[1, NE]], base=0, channel_multiplier=0, allow_small_or_imprecise_dtypes=True))
        step(gp.iota(desc_e, pattern=[[-1, NE]], base=NE, channel_multiplier=0, allow_small_or_imprecise_dtypes=True))
        step(gp.iota(invw[:, :, :], pattern=[[0, 2], [1, S]], base=1, channel_multiplier=0,
                     allow_small_or_imprecise_dtypes=True))
        gp.engine_nop().then_inc(consts, 1)
        gp.wait_ge(rel_out, 16)
        gp.dma_start(hankel[:, :, :], bass.AP(rel_pad.tensor, 1, [[1, P], [RELW, 8], [1, S]])).then_inc(hankel_in, 16)

        W = S + 16
        for l in range(2):
            if l == 1:
                gp.wait_ge(x_done, 8)
            for t, n in ((xd, 4), (pin, 16), (win_a, 16), (win_b, 16)):
                step(gp.memset(t[:, :, 0:n], 0.0))
            gp.engine_nop().then_inc(pads, 1)
            gp.wait_ge(z_out, 8 * l + 3)
            step(gp.tensor_tensor(win_a[:, :, 1:W], pin[:, :, 1:W], pin[:, :, 0:W - 1], ALU.add))
            step(gp.tensor_tensor(win_b[:, :, 2:W], win_a[:, :, 2:W], win_a[:, :, 0:W - 2], ALU.add))
            step(gp.tensor_copy(win_b[0:64, 0, :], win_a[0:64, 0, :]))
            step(gp.tensor_tensor(win_a[:, 1, 4:W], win_b[:, 1, 4:W], win_b[:, 1, 0:W - 4], ALU.add))
            step(gp.tensor_copy(win_b[0:64, 1, :], win_a[0:64, 1, :]))
            step(gp.tensor_tensor(win_b[64:P, 1, 8:W], win_a[64:P, 1, 8:W], win_a[64:P, 1, 0:W - 8], ALU.add))
            if l == 0:
                gp.wait_ge(lam_done, 1)
            else:
                gp.wait_ge(pool_ps, 1)
            step(gp.tensor_tensor(pd[:, :, :], win_b[:, :, 16:W], invw[:, :, :], ALU.mult))
            gp.tensor_tensor(pd[:, :, :], pd[:, :, :], pin[:, :, 16:W], ALU.subtract).then_inc(pool_ready, 1)
        gp.wait_ge(x_done, 12)
        diag(tri, 0, 1, [[-1, P]])
        step(gp.memset(ones[:, :], 1.0))
        step(gp.memset(tri[:, :], 1.0))
        gp.affine_select(out=tri[:, :], in_=tri[:, :], compare_op=ALU.is_gt, fill=0.0, base=0,
                         pattern=[[1, P]], channel_multiplier=-1).then_inc(consts, 1)
        gp.wait_ge(park_out, 16)
        gp.wait_ge(xn_done, 16)
        gp.memset(put[:, :, :], 0.0).then_inc(put_done, 1)
        gp.memset(x[:, :, :], 0.0).then_inc(acc_zero, 1)

    @block.scalar
    def _(act):
        next_hi = [0]

        def hi(u, slot=None, uses=None, buf=None):
            slot = u % NRING if slot is None else slot
            buf = u % NHI if buf is None else buf
            act.wait_ge(slot_in[slot], 16 * (loads(u, slot) if uses is None else uses))
            if not isinstance(u, int) or u >= NHI:
                act.wait_ge(unit_used, u - NHI + 1)
            nc.scalar.activation(w_hi[:, buf, :], slot_ap(slot), ACT.Copy).then_inc(hi_done, 1)

        def hi_to(u):
            for n in range(next_hi[0], min(u + 1, NSTATIC)):
                hi(n)
            next_hi[0] = max(next_hi[0], u + 1)

        def post_squares(n, src, junk, ready):
            for q in range(4):
                ready(q)
                if q > 1:
                    act.wait_ge(post_ssq, 4 * n + q - 1)
                nc.scalar.activation(junk(q), src(q), ACT.Square, accum_out=small[:, 12 + q:13 + q]).then_inc(post_ssq, 1)
                if q % 2:
                    t = q // 2
                    act.wait_ge(post_ms, 2 * n + t + 1)
                    nc.scalar.activation(small[:, 16 + t:17 + t], small[:, 16 + t:17 + t], ACT.Sqrt, scale=1.0 / D)\
                        .then_inc(post_root, 1)

        def pre_squares(n):
            for q in range(4):
                t = q // 2
                sl = slice(512 * (q % 2), 512 * (q % 2) + 512)
                if n == 0:
                    act.wait_ge(x_in[t], 16)
                else:
                    act.wait_ge(x_done, 4 * (n - 1) + q + 1)
                nc.scalar.activation(xn[:, t, sl], x[:, t, sl], ACT.Square, accum_out=small[:, 8 + q:9 + q]).then_inc(ssq, 1)
                if q % 2:
                    act.wait_ge(ms, 2 * n + t + 1)
                    nc.scalar.activation(small[:, 18 + t:19 + t], small[:, 18 + t:19 + t], ACT.Sqrt, scale=1.0 / D)\
                        .then_inc(root, 1)

        def h_evac(n):
            for q in range(4):
                act.wait_ge(ht_ps, 4 * n + q + 1)
                nc.scalar.activation(h_part(h_hi, q), part(bank[4 + q]), ACT.Copy).then_inc(ht_hi, 1)

        def z_evac(l, q):
            act.wait_ge(unit_used, LAYER_AT[l] + q + 1)
            b = bank[q % 2]
            v = b[:, :].rearrange("p (a s) -> p a s", a=2)
            if q == 0:
                r = nc.scalar.activation(xd[:, :, 4:S + 4], v, ACT.Copy)
            elif q == 1:
                r = nc.scalar.activation(gd[:, :, :], v, ACT.Gelu_apprx_tanh)
            elif q == 2:
                if l == 1:
                    act.wait_ge(pool_ready, 1)
                r = nc.scalar.activation(pin[:, :, 16:S + 16], v, ACT.Copy)
            elif q == 3:
                r = nc.scalar.activation(q_a[:, :, :], v, ACT.Copy, scale=HD ** -0.5)
            elif q == 4:
                nc.scalar.activation(k_a[:, :], b[:, 0:S], ACT.Copy)
                r = nc.scalar.activation(v_a[:, :, :].rearrange("p a s -> p (a s)"), b[:, S:2 * S], ACT.Copy)
            elif q == 5:
                r = nc.scalar.activation(q_c[:, :, :], v, ACT.Copy, scale=HD ** -0.5)
            elif q == 6:
                r = nc.scalar.activation(k_c[:, :, :], v, ACT.Copy)
            else:
                r = nc.scalar.activation(v_c[:, :, :], v, ACT.Copy)
            r.then_inc(z_out, 1)

        def exps(l, kind):
            bk = [bank[5], bank[6], bank[7]] if kind == "a" else [bank[0], bank[1], bank[3]]
            act.wait_ge(nmax[kind], l + 1)
            if kind == "c":
                act.wait_ge(pt_ps["a"], 3 * l + 3)
            o = 20 if kind == "a" else 36
            for t in range(TT):
                for h in range(4):
                    w = P * (t + 1)
                    b, c, n = score_at(kind, t, h)
                    r = nc.scalar.activation(probs[:, b, c:c + w], bk[b][:, c:c + w], ACT.Exp,
                                             bias=small[:, o + n:o + n + 1], accum_out=small[:, o + 8 + n:o + 9 + n])
            r.then_inc(exp_done[kind], 1)
            if kind == "a":
                act.wait_ge(sink_done, l + 1)
                nc.scalar.activation(small[:, 52:60], small[:, 52:60], ACT.Exp).then_inc(exp_done[kind], 1)

        def pt_evac(l, kind):
            bk = [bank[5], bank[6], bank[7]] if kind == "a" else [bank[0], bank[1], bank[3]]
            if kind == "c":
                act.wait_ge(pv_ps["a"], l + 1)
            for b in range(3):
                act.wait_ge(pt_ps[kind], 3 * l + b + 1)
                nc.scalar.activation(probs_t[:, b, :], bk[b][:, :], ACT.Copy).then_inc(pt_out[kind], 1)

        def y_evac_hi(l, kind):
            act.wait_ge(pv_ps[kind], l + 1)
            act.wait_ge(unit_used, LAYER_AT[l] + 8)
            k = 0 if kind == "a" else 4
            nc.scalar.activation(h_hi[:, k * S:(k + 2) * S], bank[2][:, :], ACT.Copy).then_inc(y_hi[kind], 1)

        rows = 0
        for name, pat in (("norm_mix_pre", "l (k p) -> (l k) p"), ("norm_ffn_pre", "l (k p) -> (l k) p"),
                          ("pool_scale", "l (k p) -> (l k) p"), ("conv_b", "l (k p) -> (l k) p"),
                          ("rg_b_a", "l (k p) -> (l k) p"), ("rg_b_x", "l (k p) -> (l k) p"),
                          ("rg_lambda", "l (k p) -> (l k) p"), ("conv_w", "l j (k p) -> (l j k) p")):
            src = A[name].rearrange(pat, p=P)
            act.dma_start(vrows[rows:rows + src.shape[0], :], src).then_inc(vrows_in, 16)
            rows += src.shape[0]
        assert rows == V_ROWS

        posts = [A["norm_mix_post"][0], A["norm_ffn_post"][0], A["norm_mix_post"][1]]
        pres = [A["norm_mix_pre"][0], A["norm_ffn_pre"][0], A["norm_mix_pre"][1], A["norm_ffn_pre"][1]]

        def junk(q):
            return xn[:, q // 2, 512 * (q % 2):512 * (q % 2) + 512]

        def next_pre(n):
            act.wait_ge(xn_done, 4 * n)
            act.dma_start(gpre[:, :], pres[n].partition_broadcast(P)).then_inc(gpre_in, 16)

        def next_post(n):
            act.wait_ge(x_done, 4 * n)
            act.dma_start(gpost[:, :], posts[n].partition_broadcast(P)).then_inc(gpost_in, 16)

        def block_end(last, n):
            def ready(q):
                if q < 3:
                    act.wait_ge(y_ps, 3 * n + q + 1)
                else:
                    act.wait_ge(unit_used, last + 1)
            post_squares(n, lambda q: bank[4 + q][:, :], junk, ready)
            pre_squares(n + 1)
            h_evac(n + 1)

        pre_squares(0)
        hi_to(1)
        h_evac(0)
        hi_to(3)
        act.wait_ge(lam_abs, 1)
        nc.scalar.activation(small[:, 60:64], small[:, 60:64], ACT.Exp, scale=-1.0).then_inc(lam_exp, 1)
        act.wait_ge(vec_done, 1)
        act.wait_ge(params_in, 16 * 8)
        nc.scalar.activation(rw_hi[:, :], rw[:, :, :].rearrange("p k e -> p (k e)"), ACT.Copy).then_inc(rw_hi_done, 1)
        act.wait_ge(rel_out, 16)
        for l in range(2):
            u0 = LAYER_AT[l]
            next_post(2 * l)
            next_pre(2 * l + 1)
            for q in range(6):
                hi_to(u0 + q + LEAD)
                z_evac(l, q)
                if q == 4:
                    act.wait_ge(gates_ps, l + 1)
                    for dst, b, c in ((gr, 2, V_BA), (gi, 3, V_BX)):
                        for t in range(2):
                            r = nc.scalar.activation(dst[:, t, :], bank[b][:, t * S:t * S + S], ACT.Sigmoid,
                                                     bias=vec[:, c + 2 * l + t:c + 2 * l + t + 1])
                            if dst is gr and t == 1:
                                r.then_inc(act_step, 1)
                    r.then_inc(gates_done, 1)
                    act.wait_ge(act_step, l + 1)
                    act.wait_ge(lam_done, 1)
                    for t in range(2):
                        nc.scalar.activation(th[:, t, :], gr[:, t, :], ACT.Tanh,
                                             scale=rt[:, 304 + 2 * l + t:305 + 2 * l + t])
                    for t in range(2):
                        r = nc.scalar.activation(aa[:, t, :], gr[:, t, :], ACT.Exp,
                                                 scale=rt[:, 308 + 2 * l + t:309 + 2 * l + t])
                    r.then_inc(decay_done, 1)
            hi_to(u0 + 5 + LEAD)
            exps(l, "a")
            z_evac(l, 6)
            act.wait_ge(m2_done, l + 1)
            nc.scalar.activation(th[:, :, :], th[:, :, :], ACT.Sqrt).then_inc(mult_done, 1)
            z_evac(l, 7)
            hi_to(u0 + 6 + LEAD)
            pt_evac(l, "a")
            y_evac_hi(l, "a")
            exps(l, "c")
            hi_to(u0 + 8 + LEAD)
            pt_evac(l, "c")
            hi_to(u0 + 9 + LEAD)
            y_evac_hi(l, "c")
            hi_to(u0 + 10 + LEAD)
            block_end(u0 + 11, 2 * l)
            if l == 1:
                break
            next_post(1)
            next_pre(2)
            f0 = FFN0_AT
            hi_to(f0 + LEAD)
            for j in range(FB):
                at = FFN_AT["gate", j, 1]
                hi_to(f0 + at + LEAD)
                act.wait_ge(unit_used, f0 + at + 1)
                if j > 0:
                    act.wait_ge(h_done, j)
                nc.scalar.activation(sil[:, 0:2, :].rearrange("p a s -> p (a s)"), bank[0][:, :], ACT.Silu)
                nc.scalar.activation(sil[:, 2:4, :].rearrange("p a s -> p (a s)"), bank[1][:, :], ACT.Silu)\
                    .then_inc(silu_done, 1)
                hi_to(f0 + FFN_AT["up", j, 1] + LEAD)
                act.wait_ge(h_done, j + 1)
                if j > 0:
                    act.wait_ge(unit_used, f0 + FFN_AT["down", j - 1, 1] + 1)
                nc.scalar.activation(hid_hi[:, :, :], hid[:, :, :], ACT.Copy).then_inc(hid_hi_done, 1)
            hi_to(f0 + MOE_UNITS - 2 + LEAD)
            block_end(f0 + MOE_UNITS - 1, 1)

        act.dma_start(x_park, x[:, :, :]).then_inc(park_out, 16)

        def hi_moe(i, m):
            s = moe_slot(m)
            before = loads(NSTATIC - 1, s) if s < NRING else 0
            per = MOE_UNITS // (2 * NRING)
            hi(NSTATIC + MOE_UNITS * i + m, slot=s, uses=before + per * i + m // (2 * NRING) + 1,
               buf=(NSTATIC + m) % NHI)

        def xg_evac(i):
            for b in range(2):
                act.wait_ge(gather_ps, 2 * i + b + 1)
                nc.scalar.activation(xg_hi[:, 512 * b:512 * b + 512], bank[5 + b][:, :], ACT.Copy).then_inc(xg_hi_done, 1)

        def mh_evac(i, j):
            act.wait_ge(t_done, FB * i + j + 1)
            nc.scalar.activation(mh_hi, bank[4][:, :], ACT.Copy).then_inc(hid_hi_done, 1)

        def one_pass(i, last):
            m = LEAD
            for j in range(FB):
                at = FFN_AT["gate", j, 1]
                for m in range(m, min(at + LEAD, MOE_UNITS - 1) + 1):
                    hi_moe(i, m)
                m += 1
                act.wait_ge(unit_used, NSTATIC + MOE_UNITS * i + at + 1)
                act.wait_ge(h_done, FB * (i + 1) + j)
                nc.scalar.activation(s_buf[:, :], bank[0][:, :], ACT.Silu).then_inc(silu_done, 1)
                if j > 0:
                    mh_evac(i, j - 1)
            for m in range(m, MOE_UNITS):
                hi_moe(i, m)
            if not last:
                act.wait_ge(unit_used, NSTATIC + MOE_UNITS * i + FFN_AT["up", FB - 1, 1] + 1)
                xg_evac(i + 1)
                hi_moe(i + 1, 0)
                hi_moe(i + 1, 1)
            mh_evac(i, FB - 1)
            if not last:
                for m in range(2, LEAD):
                    hi_moe(i + 1, m)

        for m in range(LEAD - 2):
            hi_moe(0, m)
        act.wait_ge(gate_arg, 1)
        nc.scalar.activation(rt[:, 64:66], rt[:, 64:66], ACT.Exp).then_inc(gate_exp, 1)
        for m in range(LEAD - 2, LEAD):
            hi_moe(0, m)
        xg_evac(0)
        for a in range(2):
            act.dma_start(glast[a][:, :], A["norm_ffn_post"][1, 512 * a:512 * a + 512].partition_broadcast(P))\
               .then_inc(glast_in, 16)
        n_pass = load_passes(act)
        last_pass = load_last(act)
        with act.Fori(0, last_pass) as i:
            one_pass(i, False)
        one_pass(last_pass, True)
        act.wait_ge(gather_ps, 2 * n_pass + 2)
        act.dma_start(xr[:, :, :], x_park).then_inc(xr_in, 16)
        post_squares(3, lambda q: x[:, q // 2, 512 * (q % 2):512 * (q % 2) + 512],
                     lambda q: xg_hi[:, 512 * (q % 2):512 * (q % 2) + 512],
                     lambda q: act.wait_ge(acc_added, 4 * n_pass + q + 1))

    @block.vector
    def _(dve):
        steps = [0]

        def step(ins):
            steps[0] += 1
            ins.then_inc(dve_step, 1)
            dve.wait_ge(dve_step, steps[0])

        V = nc.vector

        next_lo = [0]

        def lo(u, slot=None, buf=None):
            slot = u % NRING if slot is None else slot
            buf = u % NHI if buf is None else buf
            dve.wait_ge(hi_done, u + 1)
            V.tensor_tensor(ring_lo(slot), slot_ap(slot), w_hi[:, buf, :], ALU.subtract).then_inc(lo_done, 1)

        def lo_to(u):
            for n in range(next_lo[0], min(u + 1, NSTATIC)):
                lo(n)
            next_lo[0] = max(next_lo[0], u + 1)

        eps_sum = rt[:, 312:313]

        def block_norms(n, scale, res, pre):
            def mean_sum(t, at, dst, sem_in, count, sem_out):
                dve.wait_ge(sem_in, count)
                a = at + 2 * t
                V.scalar_tensor_tensor(small[:, dst + t:dst + t + 1], small[:, a:a + 1], small[:, a + 1:a + 2],
                                       eps_sum, ALU.add, ALU.add).then_inc(sem_out, 1)

            def post_sum(t):
                mean_sum(t, 12, 16, post_ssq, 4 * n + 2 * t + 2, post_ms)

            def pre_sum(t):
                mean_sum(t, 8, 18, ssq, 4 * pre + 2 * t + 2, ms)

            def inverse(t, at, sem_in, count):
                dve.wait_ge(sem_in, count)
                step(V.reciprocal(small[:, at + t:at + t + 1], small[:, at + t:at + t + 1]))

            def update(q):
                t, c = q // 2, slice(512 * (q % 2), 512 * (q % 2) + 512)
                y = bank[4 + q][:, :] if n < 3 else x[:, t, c]
                step(V.scalar_tensor_tensor(t_buf[:, :], y, small[:, 16 + t:17 + t], scale(q), ALU.mult, ALU.mult))
                V.tensor_tensor(x[:, t, c], res[:, t, c], t_buf[:, :], ALU.add).then_inc(x_done, 1)
                dve.wait_ge(x_done, 4 * n + q + 1)

            def apply(q):
                t, c = q // 2, slice(512 * (q % 2), 512 * (q % 2) + 512)
                V.scalar_tensor_tensor(xn[:, t, c], x[:, t, c], small[:, 18 + t:19 + t], gpre[:, c], ALU.mult, ALU.mult)\
                    .then_inc(xn_done, 1)

            if n is not None:
                post_sum(0)
                inverse(0, 16, post_root, 2 * n + 1)
                update(0)
                update(1)
                post_sum(1)
                inverse(1, 16, post_root, 2 * n + 2)
                update(2)
            if pre is not None:
                pre_sum(0)
            if n is not None:
                update(3)
            if pre is not None:
                inverse(0, 18, root, 2 * pre + 1)
                dve.wait_ge(gpre_in, 16 * (pre + 1))
                apply(0)
                apply(1)
                pre_sum(1)
                inverse(1, 18, root, 2 * pre + 2)
                apply(2)
                apply(3)

        def h_lows(n):
            for q in range(4):
                dve.wait_ge(ht_hi, 4 * n + q + 1)
                V.tensor_tensor(h_part(h_lo, q), part(bank[4 + q]), h_part(h_hi, q), ALU.subtract).then_inc(ht_lo, 1)

        def nmaxes(l, kind):
            bk = [bank[5], bank[6], bank[7]] if kind == "a" else [bank[0], bank[1], bank[3]]
            o = 20 if kind == "a" else 36
            for b in range(3):
                dve.wait_ge(sc_ps[kind], 3 * l + b + 1)
                n = 4 if b == 0 else 2
                at = o + (0 if b == 0 else 2 + 2 * b)
                r = V.tensor_reduce(small[:, at:at + n], bk[b][:, :].rearrange("p (h k) -> p h k", h=n), AX.X, ALU.max,
                                    negate=True)
            if kind == "c":
                r.then_inc(nmax[kind], 1)
                return
            step(r)
            sink = small[:, 4 * l:4 * l + 4]
            for t in range(TT):
                m = small[:, o + 4 * t:o + 4 * t + 4]
                r = V.scalar_tensor_tensor(m, sink, -1.0, m, ALU.mult, ALU.min)
            r.then_inc(nmax[kind], 1)
            dve.wait_ge(nmax[kind], l + 1)
            for t in range(TT):
                r = V.tensor_tensor(small[:, 52 + 4 * t:56 + 4 * t], sink, small[:, o + 4 * t:o + 4 * t + 4], ALU.add)
            r.then_inc(sink_done, 1)

        def normalise(l, kind):
            o = 20 if kind == "a" else 36
            dve.wait_ge(exp_done[kind], 2 * l + 2 if kind == "a" else l + 1)
            total = small[:, o + 8:o + 16]
            if kind == "a":
                step(V.tensor_tensor(total, total, small[:, 52:60], ALU.add))
            step(V.reciprocal(total, total))
            for t in range(TT):
                for h in range(4):
                    w = P * (t + 1)
                    b, c, n = score_at(kind, t, h)
                    r = V.tensor_scalar(probs[:, b, c:c + w], probs[:, b, c:c + w], small[:, o + 8 + n:o + 9 + n], None,
                                        ALU.mult)
            r.then_inc(prob_done[kind], 1)

        def y_evac_lo(l, kind):
            dve.wait_ge(y_hi[kind], l + 1)
            k = 0 if kind == "a" else 4
            V.tensor_tensor(h_lo[:, k * S:(k + 2) * S], bank[2][:, :], h_hi[:, k * S:(k + 2) * S], ALU.subtract)\
                .then_inc(y_lo[kind], 1)

        step(V.memset(eps_sum, D * EPS))
        block_norms(None, None, None, 0)
        lo_to(1)
        h_lows(0)
        lo_to(3)
        dve.wait_ge(rel_in, 16)
        V.tensor_copy(relrow[:, 2 * RELCLIP + 1:RELW],
                      relrow[:, 2 * RELCLIP:2 * RELCLIP + 1].to_broadcast([8, RELW - 2 * RELCLIP - 1])).then_inc(rel_row, 1)
        dve.wait_ge(vec_ps, 1)
        V.tensor_copy(vec[:, :], bank[0][:, 0:V_ROWS]).then_inc(vec_done, 1)
        dve.wait_ge(vec_done, 1)
        lam = vec[:, V_LAM:V_LAM + 4]
        y, z, z2, p = (rt[:, 4 * a:4 * a + 4] for a in range(4))
        step(V.tensor_scalar(y, lam, -1.0, None, ALU.mult))
        V.tensor_tensor(small[:, 60:64], lam, y, ALU.max).then_inc(lam_abs, 1)
        dve.wait_ge(lam_exp, 1)
        step(V.tensor_scalar(z, small[:, 60:64], 2.0, None, ALU.add))
        step(V.reciprocal(z, z))
        step(V.tensor_tensor(z, z, small[:, 60:64], ALU.mult))
        step(V.tensor_tensor(z2, z, z, ALU.mult))
        step(V.tensor_scalar(p, z2, 1.0 / 17, None, ALU.mult))
        for n in (15, 13, 11, 9, 7, 5, 3):
            step(V.scalar_tensor_tensor(p, p, 1.0 / n, z2, ALU.add, ALU.mult))
        step(V.scalar_tensor_tensor(p, p, 1.0, z, ALU.add, ALU.mult))
        step(V.tensor_scalar(y, y, 0.0, None, ALU.max))
        step(V.scalar_tensor_tensor(p, p, 2.0, y, ALU.mult, ALU.add))
        step(V.tensor_scalar(rt[:, 304:308], p, 8.0, None, ALU.mult))
        step(V.tensor_scalar(rt[:, 308:312], p, -8.0, None, ALU.mult))
        dve.wait_ge(consts, 2)
        for t, c, w in ((0, 0, 2.0), (0, 64, 4.0), (1, 0, 8.0), (1, 64, 16.0)):
            r = V.tensor_scalar(invw[c:c + 64, t, :], invw[c:c + 64, t, :], w, None, ALU.min)
        step(r)
        inverted = V.reciprocal(invw[:, :, :], invw[:, :, :])
        inverted.then_inc(lam_done, 1)

        dve.wait_ge(rw_hi_done, 1)
        V.tensor_tensor(rw_lo[:, :], rw[:, :, :].rearrange("p k e -> p (k e)"), rw_hi[:, :], ALU.subtract).then_inc(rw_lo_done, 1)

        for l in range(2):
            u0 = LAYER_AT[l]
            lo_to(u0 + LEAD)
            dve.wait_ge(z_out, 8 * l + 1)
            dve.wait_ge(pads, l + 1)
            for j in (3, 2, 1, 0):
                for t in range(2):
                    c = V_CONVW + (l * 4 + j) * 2 + t
                    src = xd[:, t, j + 1:j + 1 + S]
                    if j == 3:
                        b = V_CONVB + 2 * l + t
                        r = V.tensor_scalar(xc[:, t, :], src, vec[:, c:c + 1], vec[:, b:b + 1], ALU.mult, ALU.add)
                    else:
                        r = V.scalar_tensor_tensor(xc[:, t, :], src, vec[:, c:c + 1], xc[:, t, :], ALU.mult, ALU.add)
                if j:
                    step(r)
            r.then_inc(conv_done, 1)
            lo_to(u0 + 4 + LEAD)
            dve.wait_ge(decay_done, l + 1)
            V.tensor_tensor(gi[:, :, :], gi[:, :, :], xc[:, :, :], ALU.mult)
            step(V.tensor_tensor(gr[:, :, :], aa[:, :, :], aa[:, :, :], ALU.mult))
            V.scalar_tensor_tensor(th[:, :, :], gr[:, :, :], 1.0, th[:, :, :], ALU.add, ALU.mult).then_inc(m2_done, 1)
            lo_to(u0 + 5 + LEAD)
            nmaxes(l, "a")
            normalise(l, "a")
            dve.wait_ge(mult_done, l + 1)
            step(V.tensor_tensor(gi[:, :, :], gi[:, :, :], th[:, :, :], ALU.mult))
            for t in range(2):
                r = V.tensor_tensor_scan(gr[:, t, :], aa[:, t, :], gi[:, t, :], 0.0, ALU.mult, ALU.add)
            step(r)
            step(V.tensor_tensor(gd[:, :, :], gd[:, :, :], gr[:, :, :], ALU.mult))
            lo_to(u0 + 6 + LEAD)
            dve.wait_ge(pool_ps, l + 1)
            dve.wait_ge(unit_used, u0 + 8)
            for t in range(2):
                sl = slice((2 + t) * S, (3 + t) * S)
                c = V_PSCALE + 2 * l + t
                step(V.tensor_scalar(h_hi[:, sl], bank[4][:, t * S:t * S + S], vec[:, c:c + 1], None, ALU.mult))
                r = V.scalar_tensor_tensor(h_lo[:, sl], bank[4][:, t * S:t * S + S], vec[:, c:c + 1], h_hi[:, sl],
                                           ALU.mult, ALU.subtract)
            r.then_inc(yb_done, 1)
            sl = slice(6 * S, 8 * S)
            gdf = gd[:, :, :].rearrange("p a s -> p (a s)")
            step(V.tensor_copy(h_hi[:, sl], gdf))
            V.tensor_tensor(h_lo[:, sl], gdf, h_hi[:, sl], ALU.subtract).then_inc(yd_done, 1)
            nmaxes(l, "c")
            y_evac_lo(l, "a")
            normalise(l, "c")
            lo_to(u0 + 9 + LEAD)
            y_evac_lo(l, "c")
            lo_to(u0 + 10 + LEAD)
            dve.wait_ge(gpost_in, 16 * (2 * l + 1))

            def gpost_part(q):
                return gpost[:, 512 * (q % 2):512 * (q % 2) + 512]

            block_norms(2 * l, gpost_part, x, 2 * l + 1)
            h_lows(2 * l + 1)
            if l == 1:
                break
            f0 = FFN0_AT
            lo_to(f0 + LEAD)
            for j in range(FB):
                at = FFN_AT["up", j, 1]
                lo_to(f0 + at + LEAD - 1)
                dve.wait_ge(silu_done, j + 1)
                dve.wait_ge(unit_used, f0 + at + 1)
                if j > 0:
                    dve.wait_ge(hid_lo_done, j)
                for a in range(2):
                    r = V.tensor_tensor(hid[:, 2 * a:2 * a + 2, :].rearrange("p a s -> p (a s)"),
                                        sil[:, 2 * a:2 * a + 2, :].rearrange("p a s -> p (a s)"),
                                        bank[2 + a][:, :], ALU.mult)
                r.then_inc(h_done, 1)
                lo_to(f0 + at + LEAD)
                dve.wait_ge(hid_hi_done, j + 1)
                V.tensor_tensor(hid_lo[:, :, :], hid[:, :, :], hid_hi[:, :, :], ALU.subtract).then_inc(hid_lo_done, 1)
            lo_to(f0 + MOE_UNITS - 2 + LEAD)
            dve.wait_ge(gpost_in, 32)
            block_norms(1, gpost_part, x, 2)
            h_lows(2)

        def lo_moe(i, m):
            lo(NSTATIC + MOE_UNITS * i + m, slot=moe_slot(m), buf=(NSTATIC + m) % NHI)

        def r3(at):
            return rt[:, at:at + 16].rearrange("p (t e) -> p t e", t=TT)

        def bc(ap):
            return ap.unsqueeze(2).to_broadcast([P, TT, NE])

        def bce(ap):
            return ap.unsqueeze(1).to_broadcast([P, TT, NE])

        lg, eq, oh1, oh2, g, sel = (r3(16 * a) for a in range(5 + 1))
        stab = rt[:, 96:120].rearrange("p (t c) -> p t c", t=TT)
        gtab = rt[:, 120:144].rearrange("p (t c) -> p t c", t=TT)
        m1, mx, m2, den = (rt[:, 144 + 2 * a:146 + 2 * a] for a in range(4))
        cnt, over, order = rt[:, 152:160], rt[:, 160:168], rt[:, 168:176]
        selx = rt[:, 176:200].rearrange("p (i e) -> p i e", i=MAX_EXTRA)
        tmpx = rt[:, 200:224].rearrange("p (i e) -> p i e", i=MAX_EXTRA)
        lst = rt[:, 224:229]
        arg = rt[:, 64:66]

        dve.wait_ge(logit_ps, 1)
        step(V.tensor_copy(lg, bank[0][:, 0:TT * NE].rearrange("p (t e) -> p t e", t=TT)))

        def one_hot(dst, src, top):
            step(V.tensor_reduce(top, src, AX.X, ALU.max))
            step(V.tensor_tensor(eq, src, bc(top), ALU.is_equal))
            step(V.tensor_tensor(sel, eq, bce(desc_e), ALU.mult))
            step(V.tensor_reduce(mx, sel, AX.X, ALU.max))
            step(V.tensor_tensor(dst, sel, bc(mx), ALU.is_equal))

        one_hot(oh1, lg, m1)
        step(V.scalar_tensor_tensor(lg, oh1, -3.0e38, lg, ALU.mult, ALU.add))
        one_hot(oh2, lg, m2)
        V.tensor_tensor(arg, m2, m1, ALU.subtract).then_inc(gate_arg, 1)
        V.tensor_tensor(sel, oh1, oh2, ALU.add).then_inc(taken, 1)
        lo_moe(0, 0)
        dve.wait_ge(gate_exp, 1)
        step(V.tensor_copy(mx, arg))
        step(V.tensor_scalar(den, mx, 1.0, None, ALU.add))
        step(V.reciprocal(den, den))
        step(V.tensor_tensor(mx, mx, den, ALU.mult))
        step(V.tensor_tensor(oh1, oh1, bc(den), ALU.mult))
        step(V.tensor_tensor(oh2, oh2, bc(mx), ALU.mult))
        step(V.memset(stab, NO_SLOT))
        step(V.memset(gtab, 0.0))
        step(V.tensor_tensor(gtab[:, :, 0:NE], oh1, oh2, ALU.add))
        dve.wait_ge(rank_ps, 1)
        step(V.tensor_scalar(eq, sel, -NO_SLOT, NO_SLOT, ALU.mult, ALU.add))
        step(V.tensor_tensor(stab[:, :, 0:NE], eq, bank[1][:, 0:TT * NE].rearrange("p (t e) -> p t e", t=TT), ALU.add))
        for t in range(TT):
            r = V.tensor_scalar(pick[:, t, :], iota_row[:, :], stab[:, t, 0:1], None, ALU.is_equal)
        r.then_inc(p_done, 1)
        lo_moe(0, 1)
        step(V.tensor_copy(cnt, bank[1][:, TT * NE:(TT + 1) * NE]))
        step(V.tensor_scalar(over, cnt, float(P), None, ALU.is_gt))
        step(V.memset(cnt, 1.0))
        step(V.tensor_tensor_scan(order, cnt, over, 0.0, ALU.mult, ALU.add))
        for i in range(MAX_EXTRA):
            step(V.scalar_tensor_tensor(selx[:, i, :], order, float(i + 1), over, ALU.is_equal, ALU.mult))
        for t in range(TT):
            for tab, shift in ((stab, -float(P)), (gtab, 0.0)):
                src = tab[:, t, 0:NE].unsqueeze(1).to_broadcast([P, MAX_EXTRA, NE])
                step(V.tensor_tensor(tmpx, selx, src, ALU.mult))
                step(V.tensor_reduce(lst[:, 0:MAX_EXTRA], tmpx, AX.X, ALU.add))
                step(V.tensor_scalar(tab[:, t, NE:NE + MAX_EXTRA], lst[:, 0:MAX_EXTRA], shift, None, ALU.add))
        step(V.tensor_tensor(tmpx, selx, iota_e.unsqueeze(1).to_broadcast([P, MAX_EXTRA, NE]), ALU.mult))
        step(V.tensor_reduce(lst[:, 1:1 + MAX_EXTRA], tmpx, AX.X, ALU.add))
        step(V.tensor_scalar(lst[:, 0:1], order[:, NE - 1:NE], float(NE), None, ALU.add))
        step(V.tensor_scalar(lst[:, 4:5], order[:, NE - 1:NE], float(NE - 1), None, ALU.add))
        V.tensor_copy(ev[0:1, 0:5], lst[0:1, :]).then_inc(tables, 1)

        def picks(i):
            for t in range(TT):
                r = V.tensor_scalar(pick[:, t, :], iota_row[:, :], stab[:, t, bass.ds(i, 1)], None, ALU.is_equal)
            r.then_inc(p_done, 1)

        def xg_lows(i):
            for b in range(2):
                dve.wait_ge(xg_hi_done, 2 * i + b + 1)
                V.tensor_tensor(xg_lo[:, 512 * b:512 * b + 512], bank[5 + b][:, :], xg_hi[:, 512 * b:512 * b + 512],
                                ALU.subtract).then_inc(xg_lo_done, 1)

        def y_out(i):
            dve.wait_ge(unit_used, NSTATIC + MOE_UNITS * i)
            for a in range(2):
                r = V.tensor_copy(y_slots[:, 512 * a:512 * a + 512], bank[2 + a][:, :])
            r.then_inc(y_evac, 1)

        def add_scatter(i):
            for q in range(4):
                dve.wait_ge(scatter_ps, 4 * i + q + 1)
                sl = x[:, q // 2, 512 * (q % 2):512 * (q % 2) + 512]
                V.tensor_tensor(sl, sl, bank[[5, 6, 7, 4][q]][:, :], ALU.add).then_inc(acc_added, 1)

        def mh_low(i, j):
            dve.wait_ge(hid_hi_done, FB * (i + 1) + j + 1)
            V.tensor_tensor(mh_lo, bank[4][:, :], mh_hi, ALU.subtract).then_inc(hid_lo_done, 1)

        def one_pass(i, last):
            m = LEAD
            y_out(i)
            for j in range(FB):
                at = FFN_AT["up", j, 1]
                for m in range(m, min(at + LEAD - 1, MOE_UNITS - 1) + 1):
                    lo_moe(i, m)
                    if j > 0 and m == FFN_AT["gate", j, 1] + LEAD:
                        mh_low(i, j - 1)
                m += 1
                dve.wait_ge(silu_done, FB * (i + 1) + j + 1)
                dve.wait_ge(unit_used, NSTATIC + MOE_UNITS * i + at + 1)
                if j > 0:
                    dve.wait_ge(t_done, FB * i + j)
                V.tensor_tensor(t_buf[:, :], s_buf[:, :], bank[1][:, :], ALU.mult).then_inc(h_done, 1)
                if j == 0:
                    add_scatter(i)
                    dve.wait_ge(gather_ps, 2 * i + 2)
                    picks(i + 1)
                    for t in range(TT):
                        r = V.tensor_scalar(pickg[:, t, :], iota_row[:, :], stab[:, t, bass.ds(i, 1)],
                                            gtab[:, t, bass.ds(i, 1)], ALU.is_equal, ALU.mult)
                    r.then_inc(pg_done, 1)
                if j == 4:
                    dve.wait_ge(put_ps, i + 1)
                    V.tensor_copy(put[:, :, :].rearrange("p t s -> p (t s)"), bank[7][:, 0:TT * P]).then_inc(put_done, 1)
            if not last:
                xg_lows(i + 1)
                lo_moe(i + 1, 0)
                lo_moe(i + 1, 1)
            mh_low(i, FB - 1)
            if not last:
                for m in range(2, LEAD):
                    lo_moe(i + 1, m)

        for m in range(2, LEAD):
            lo_moe(0, m)
        xg_lows(0)
        dve.wait_ge(acc_zero, 1)
        dve.wait_ge(y_zero, 1)
        n_pass = load_passes(dve)
        last_pass = load_last(dve)
        with dve.Fori(0, last_pass) as i:
            one_pass(i, False)
        one_pass(last_pass, True)
        y_out(n_pass)
        add_scatter(n_pass)
        dve.wait_ge(xr_in, 16)
        dve.wait_ge(glast_in, 32)
        block_norms(3, lambda q: glast[q % 2][:, :], xr, None)

    @block.tensor
    def _(pe):
        T = nc.tensor

        def split_mm(dst, l_hi, l_lo, r_hi, r_lo, first, last):
            T.matmul(dst, l_lo, r_hi, start=first, stop=False, skip_group_check=True)
            T.matmul(dst, l_hi, r_lo, start=False, stop=False, skip_group_check=True)
            return T.matmul(dst, l_hi, r_hi, start=False, stop=last, skip_group_check=True)

        pairs = [0]

        def ht(k, c, n):
            return slice(k * S + c, k * S + c + n)

        def transpose_h(n):
            for q in range(4):
                t, k0 = q // 2, 4 * (q % 2)
                pe.wait_ge(xn_done, 4 * n + q + 1)
                for k in range(4):
                    r = T.transpose(bank[4 + q][:, k * P:k * P + P], xn[:, t, (k0 + k) * P:(k0 + k) * P + P], ident[:, :])
                r.then_inc(ht_ps, 1)

        def h_wait(n, k):
            pe.wait_ge(ht_lo, 4 * n + 3 + k // 4)

        def block_quarter(r, q):
            if q < 3:
                r.then_inc(y_ps, 1)

        def w_in(l, q):
            u = LAYER_AT[l] + q
            c = WIN_ORDER[q]
            buf = u % NHI
            wh = w_hi[:, buf, :].rearrange("p (k c) -> p k c", c=256)
            wl = ring_lo(u % NRING).rearrange("p (k c) -> p k c", c=256)
            pe.wait_ge(lo_done, u + 1)
            if q >= 2:
                pe.wait_ge(z_out, 8 * l + q - 1)
            dst = bank[q % 2]
            for a in range(2):
                if c == 5 or (c == 1 and a == 1):
                    continue
                for k in range(KT):
                    if q == 0 and a == 0 and k % 4 == 0:
                        h_wait(2 * l, k)
                    lh, ll = wh[:, k, a * P:a * P + P], wl[:, k, a * P:a * P + P]
                    r = split_mm(dst[:, a * S:a * S + S], lh, ll, h_hi[:, ht(k, 0, S)], h_lo[:, ht(k, 0, S)],
                                 k == 0, k == KT - 1)
            if c in (1, 5):
                n, c0 = (P, P) if c == 1 else (S, 0)
                o = S if c == 1 else 0
                for t in range(TT):
                    for k in range(KT):
                        r = split_mm(dst[:, o + t * n:o + t * n + n], h_hi[:, ht(k, t * P, P)], h_lo[:, ht(k, t * P, P)],
                                     wh[:, k, c0:c0 + n], wl[:, k, c0:c0 + n], k == 0, k == KT - 1)
            r.then_inc(unit_used, 1)

        def blocks(dst, w, l, src):
            for n in range(4):
                rows = slice(HD * (n % 2), HD * (n % 2) + HD)
                r = T.matmul(dst[rows, (n // 2) * S:(n // 2) * S + S], w[rows, l, n // 2, :], src[rows, n // 2, :],
                             start=True, stop=True)
            return r

        def scores(l, kind):
            bk = [bank[5], bank[6], bank[7]] if kind == "a" else [bank[0], bank[1], bank[3]]
            for t in range(TT):
                m = mask_t0 if t == 0 else mask_a1 if kind == "a" else mask_c1
                for pair in range(2):
                    rows = slice(HD * pair, HD * pair + HD)
                    for n in range(2):
                        h = 2 * pair + n if kind == "a" else 2 * n + pair
                        w = P * (t + 1)
                        b, c, _ = score_at(kind, t, h)
                        dst = bk[b][:, c:c + w]
                        q, k = (q_a[rows, n, :], k_a[rows, :]) if kind == "a" else (q_c[rows, n, :], k_c[rows, n, :])
                        T.matmul(dst, q[:, t * P:t * P + P], k[:, 0:w], start=True, stop=False)
                        r = T.matmul(dst, chunk_l[rows, :], m[rows, 0:w], start=False, stop=(kind == "a"))
                        for kt in range(t + 1 if kind == "c" else 0):
                            j = P * (t - kt)
                            r = T.matmul(bk[b][:, c + kt * P:c + kt * P + P], hankel[:, 4 * l + h, j:j + P], flip[:, :],
                                         start=False, stop=(kt == t))
                    if t == 0 and pair == 0:
                        r.then_inc(pe_pair, 1)
                        pairs[0] += 1
                        pe.wait_ge(pe_pair, pairs[0])
                    else:
                        r.then_inc(sc_ps[kind], 1)

        def transposes(l, kind):
            bk = [bank[5], bank[6], bank[7]] if kind == "a" else [bank[0], bank[1], bank[3]]
            pe.wait_ge(prob_done[kind], l + 1)
            for g in range(3):
                for h in range(4):
                    b, c, _ = score_at(kind, min(g, 1), h)
                    c += P * (g == 2)
                    r = T.transpose(bk[g][:, h * P:h * P + P], probs[:, b, c:c + P], ident[:, :])
                r.then_inc(pt_ps[kind], 1)

        def values(l, kind):
            pe.wait_ge(pt_out[kind], 3 * l + 3)
            if kind == "c":
                pe.wait_ge(y_lo["a"], l + 1)
            for h in range(4):
                rows = slice(HD * (h % 2), HD * (h % 2) + HD)
                for t in range(TT):
                    for kt in range(t + 1):
                        v = v_a[:, kt, HD * (h // 2):HD * (h // 2) + HD] if kind == "a" else v_c[:, kt, HD * h:HD * h + HD]
                        r = T.matmul(bank[2][rows, (h // 2) * S + t * P:(h // 2) * S + t * P + P], v,
                                     probs_t[:, t + kt, h * P:h * P + P], start=(kt == 0), stop=(kt == t))
            r.then_inc(pv_ps[kind], 1)

        def w_out(l, n):
            u = LAYER_AT[l] + 8 + n
            k0 = 2 * WOUT_ORDER[n]
            buf = u % NHI
            pe.wait_ge(lo_done, u + 1)
            pe.wait_ge([yb_done, yd_done, y_lo["a"], y_lo["c"]][n], l + 1)
            for t in range(TT):
                for a in range(2):
                    for k in range(2):
                        c = k * D + 512 * a
                        r = split_mm(bank[4 + 2 * t + a][:, :], h_hi[:, ht(k0 + k, t * P, P)], h_lo[:, ht(k0 + k, t * P, P)],
                                     w_hi[:, buf, c:c + 512], ring_lo(u % NRING)[:, c:c + 512],
                                     n == 0 and k == 0, n == 3 and k == 1)
                    if n == 3:
                        block_quarter(r, 2 * t + a)
            r.then_inc(unit_used, 1)

        pe.wait_ge(consts, 1)
        transpose_h(0)
        pe.wait_ge(vrows_in, 16 * 8)
        T.transpose(bank[0][:, 0:V_ROWS], vrows[:, :], ident[0:V_ROWS, 0:V_ROWS]).then_inc(vec_ps, 1)
        pe.wait_ge(vec_done, 1)
        for l in range(2):
            for q in range(4):
                w_in(l, q)
            pe.wait_ge(conv_done, l + 1)
            pe.wait_ge(params_in, 16 * 8)
            blocks(bank[2], rg_wa, l, xc)
            blocks(bank[3], rg_wx, l, xc).then_inc(gates_ps, 1)
            w_in(l, 4)
            w_in(l, 5)
            pe.wait_ge(consts, 2)
            pe.wait_ge(z_out, 8 * l + 5)
            scores(l, "a")
            pe.wait_ge(pool_ready, l + 1)
            blocks(bank[4], pool_w, l, pd).then_inc(pool_ps, 1)
            w_in(l, 6)
            w_in(l, 7)
            transposes(l, "a")
            pe.wait_ge(hankel_in, 16)
            pe.wait_ge(z_out, 8 * l + 8)
            pe.wait_ge(gates_done, l + 1)
            scores(l, "c")
            values(l, "a")
            w_out(l, 0)
            w_out(l, 1)
            transposes(l, "c")
            w_out(l, 2)
            values(l, "c")
            w_out(l, 3)
            transpose_h(2 * l + 1)
            if l == 1:
                break
            f0 = FFN0_AT
            for j in range(FB + 1):
                if j < FB:
                    for kind, b0, free in (("gate", 0, silu_done), ("up", 2, h_done)):
                        for b in range(2):
                            u = f0 + FFN_AT[kind, j, b]
                            buf = u % NHI
                            pe.wait_ge(lo_done, u + 1)
                            if j > 0 and b == 0:
                                pe.wait_ge(free, j)
                            for f in range(4):
                                if j == 0 and kind == "gate" and f == 0:
                                    h_wait(1, 4 * b)
                                for k in range(4):
                                    c = k * 512 + f * P
                                    kk = 4 * b + k
                                    r = split_mm(bank[b0 + f // 2][:, (f % 2) * S:(f % 2) * S + S],
                                                 w_hi[:, buf, c:c + P], ring_lo(u % NRING)[:, c:c + P],
                                                 h_hi[:, ht(kk, 0, S)], h_lo[:, ht(kk, 0, S)],
                                                 kk == 0 and f % 2 == 0, kk == KT - 1)
                            r.then_inc(unit_used, 1)
                if j > 0:
                    for b in range(2):
                        u = f0 + FFN_AT["down", j - 1, b]
                        buf = u % NHI
                        pe.wait_ge(lo_done, u + 1)
                        pe.wait_ge(hid_lo_done, j)
                        for t in range(TT):
                            for a in range(2):
                                for f in range(2):
                                    c = f * D + 512 * a
                                    ff = 2 * b + f
                                    r = split_mm(bank[4 + 2 * t + a][:, :], hid_hi[:, ff, t * P:t * P + P],
                                                 hid_lo[:, ff, t * P:t * P + P], w_hi[:, buf, c:c + 512],
                                                 ring_lo(u % NRING)[:, c:c + 512], j == 1 and ff == 0,
                                                 j == FB and ff == 3)
                                if j == FB and b == 1:
                                    block_quarter(r, 2 * t + a)
                        r.then_inc(unit_used, 1)
            transpose_h(2)

        pe.wait_ge(rw_lo_done, 1)
        for t in range(TT):
            pe.wait_ge(ht_lo, 14 + 2 * t)
            for k in range(KT):
                r = split_mm(bank[0][:, t * NE:t * NE + NE], h_hi[:, ht(k, t * P, P)], h_lo[:, ht(k, t * P, P)],
                             rw_hi[:, k * NE:k * NE + NE], rw_lo[:, k * NE:k * NE + NE], k == 0, k == KT - 1)
        r.then_inc(logit_ps, 1)
        pe.wait_ge(consts, 3)
        pe.wait_ge(taken, 1)
        m = rt[:, 80:96].rearrange("p (t e) -> p t e", t=TT)
        T.matmul(bank[1][:, 0:NE], tri[:, :], m[:, 0, :], start=True, stop=True)
        T.matmul(bank[1][:, NE:2 * NE], ones[:, :], m[:, 0, :], start=True, stop=False)
        T.matmul(bank[1][:, NE:2 * NE], tri[:, :], m[:, 1, :], start=False, stop=True)
        T.matmul(bank[1][:, 2 * NE:3 * NE], ones[:, :], m[:, 0, :], start=True, stop=False)
        T.matmul(bank[1][:, 2 * NE:3 * NE], ones[:, :], m[:, 1, :], start=False, stop=True).then_inc(rank_ps, 1)

        def gather():
            for b in range(2):
                for a in range(4):
                    k = 4 * b + a
                    for t in range(TT):
                        r = T.matmul(bank[5 + b][:, a * P:a * P + P], xn[:, t, k * P:k * P + P], pick[:, t, :],
                                     start=(t == 0), stop=(t == TT - 1))
                r.then_inc(gather_ps, 1)

        def scatter(i):
            pe.wait_ge(y_evac, i + 1)
            pe.wait_ge(put_done, i + 1)
            for q in range(4):
                if q == 3:
                    pe.wait_ge(hid_lo_done, FB * (i + 1))
                T.matmul(bank[[5, 6, 7, 4][q]][:, :], put[:, q // 2, :], y_slots[:, 512 * (q % 2):512 * (q % 2) + 512],
                         start=True, stop=True).then_inc(scatter_ps, 1)

        def unit_wait(i, unit):
            m = FFN_AT[unit]
            pe.wait_ge(lo_done, NSTATIC + MOE_UNITS * i + m + 1)
            return (NSTATIC + m) % NHI, ring_lo(moe_slot(m))

        def up_proj(i, j, kind, dst, free):
            for b in range(2):
                buf, w_lo = unit_wait(i, (kind, j, b))
                if b == 0:
                    pe.wait_ge(free, FB * (i + 1) + j)
                for k in range(4):
                    kk = 4 * b + k
                    r = split_mm(dst[:, :], xg_hi[:, kk * P:kk * P + P], xg_lo[:, kk * P:kk * P + P],
                                 w_hi[:, buf, k * 512:k * 512 + 512], w_lo[:, k * 512:k * 512 + 512],
                                 kk == 0, kk == KT - 1)
                r.then_inc(unit_used, 1)

        def turn(i, j):
            pe.wait_ge(h_done, FB * (i + 1) + j + 1)
            pe.wait_ge(hid_lo_done, FB * (i + 1) + j)
            if j == 0:
                pe.wait_ge(acc_added, 4 * i + 4)
            for f in range(4):
                r = T.transpose(bank[4][:, f * P:f * P + P], t_buf[:, f * P:f * P + P], ident[:, :])
            r.then_inc(t_done, 1)

        def down_proj(i, j):
            pe.wait_ge(hid_lo_done, FB * (i + 1) + j + 1)
            if j == 0:
                pe.wait_ge(y_evac, i + 1)
            for b in range(2):
                buf, w_lo = unit_wait(i, ("down", j, b))
                for f in range(2):
                    ff = 2 * b + f
                    for a in range(2):
                        c = f * D + 512 * a
                        r = split_mm(bank[2 + a][:, :], mh_hi[:, ff * P:ff * P + P], mh_lo[:, ff * P:ff * P + P],
                                     w_hi[:, buf, c:c + 512], w_lo[:, c:c + 512],
                                     j == 0 and ff == 0, j == FB - 1 and ff == 3)
                r.then_inc(unit_used, 1)
            return r

        pe.wait_ge(put_done, 1)
        for a in range(2):
            r = T.matmul(bank[2 + a][:, 0:TT * P], put[:, 0, :], put[:, :, :].rearrange("p t s -> p (t s)"),
                         start=True, stop=True)
            r = T.matmul(bank[2 + a][:, TT * P:512], put[:, 0, :], put[:, :, :].rearrange("p t s -> p (t s)"),
                         start=True, stop=True)
        r.then_inc(y_zero, 1)
        pe.wait_ge(p_done, 1)
        gather()
        n_pass = load_passes(pe)
        with pe.Fori(0, n_pass) as i:
            pe.wait_ge(xg_lo_done, 2 * i + 2)
            for j in range(FB):
                up_proj(i, j, "gate", bank[0], silu_done)
                if j > 0:
                    turn(i, j - 1)
                up_proj(i, j, "up", bank[1], h_done)
                if j == 0:
                    scatter(i)
                if j == 3:
                    pe.wait_ge(pg_done, i + 1)
                    for t in range(TT):
                        r = T.transpose(bank[7][:, t * P:t * P + P], pickg[:, t, :], ident[:, :])
                    r.then_inc(put_ps, 1)
                if j == 5:
                    pe.wait_ge(p_done, i + 2)
                    gather()
                if j > 0:
                    down_proj(i, j - 1)
            turn(i, FB - 1)
            down_proj(i, FB - 1)
        scatter(n_pass)

    block.__exit__(None, None, None)


_INS = ["x", "norm_mix_pre", "w_in", "attn_sinks", "pool_w", "pool_scale", "rel_bias", "conv_w", "conv_b",
        "rg_w_a", "rg_b_a", "rg_w_x", "rg_b_x", "rg_lambda", "w_out", "norm_mix_post", "norm_ffn_pre",
        "norm_ffn_post", "ffn_w_gate", "ffn_w_up", "ffn_w_down", "router_w", "moe_w_gate", "moe_w_up", "moe_w_down"]


def kernel(**inputs):
    import numpy as np
    import concourse.bacc as bacc
    from concourse.bass_utils import run_bass_kernel_spmd

    nc = bacc.Bacc("TRN2", target_bir_lowering=False, num_devices=1)
    arrays, args = {}, {}
    for name in _INS:
        a = np.ascontiguousarray(inputs[name])
        arrays[f"in_{name}"] = a
        args[name] = nc.dram_tensor(f"in_{name}", a.shape, mybir.dt.from_np(a.dtype), kind="ExternalInput").ap()
    out = nc.dram_tensor("out_x", (1, S, D), F32, kind="ExternalOutput").ap()
    build(nc, args, out)
    return run_bass_kernel_spmd(nc, [arrays], core_ids=[0]).results[0]["out_x"]
```

```python
import concourse.bass as bass
from concourse import mybir

F32 = mybir.dt.float32
F32R = mybir.dt.float32r
BF16 = mybir.dt.bfloat16
I32 = mybir.dt.int32
ALU = mybir.AluOpType
ACT = mybir.ActivationFunctionType
AX = mybir.AxisListType

P = 128
S = 256
TT = S // P
D = 1024
KT = D // P
FF = 3584
FB = FF // 512
NE = 8
HD = 64
EPS = 1e-6
NEG = -1e30
RELCLIP = 128
RELW = 384
UNIT = 2048
NRING = 7
NHI = 6
LEAD = 5
MOE_UNITS = 6 * FB
MAX_EXTRA = 3
NO_SLOT = 1000.0
WIN_ORDER = [6, 7, 2, 0, 1, 3, 4, 5]
WOUT_ORDER = [1, 3, 0, 2]
V_PSCALE, V_CONVB, V_BA, V_BX, V_LAM, V_CONVW, V_ROWS = 0, 4, 8, 12, 16, 20, 36


def ffn_units():
    out = []
    for j in range(FB + 1):
        if j < FB:
            out += [("gate", j, 0), ("gate", j, 1), ("up", j, 0), ("up", j, 1)]
        if j > 0:
            out += [("down", j - 1, 0), ("down", j - 1, 1)]
    return out


FFN_UNITS = ffn_units()
FFN_AT = {u: n for n, u in enumerate(FFN_UNITS)}
MIX_UNITS = [("win", c, 0) for c in WIN_ORDER] + [("wout", r, 0) for r in WOUT_ORDER]
STATIC = [(0, u) for u in MIX_UNITS + FFN_UNITS] + [(1, u) for u in MIX_UNITS]
NSTATIC = len(STATIC)
LAYER_AT = [0, len(MIX_UNITS) + MOE_UNITS]
FFN0_AT = len(MIX_UNITS)


def loads(u, slot):
    return sum(4 if STATIC[n][1] == ("win", 0, 0) else 1 for n in range(u + 1) if n % NRING == slot)


def moe_slot(m):
    order = [(NSTATIC + s) % NRING for s in range(3)] + list(range(NRING, 2 * NRING))
    order += [(NSTATIC + s) % NRING for s in range(3, NRING)]
    return order[m % (2 * NRING)]


def build(nc, A, out):
    base = -(-nc.sbuf_base // 64) * 64
    place = [base]

    def sb(name, shape, dt=F32, at=None):
        size = 2 if dt == BF16 else 4
        for n in shape[1:]:
            size *= n
        off = place[0] if at is None else at
        if at is None:
            place[0] += -(-size // 32) * 32
        return nc.alloc_sbuf_tensor_at(name, shape, dt, offset=off)

    ring_a = sb("ring_a", [P, NRING, UNIT])
    ring_a_lo = sb("ring_a_lo", [P, NRING, UNIT], F32R, at=base)
    mix_base = place[0]
    ring_b = sb("ring_b", [P, NRING, UNIT])
    ring_b_lo = sb("ring_b_lo", [P, NRING, UNIT], F32R, at=mix_base)
    mix_end = place[0]
    w_hi = sb("w_hi", [P, NHI, UNIT], F32R)
    x_at = place[0]
    x = sb("x", [P, TT, D])
    hhi_at = place[0]
    h_hi = sb("h_hi", [P, KT * S], F32R)
    hlo_at = place[0]
    h_lo = sb("h_lo", [P, KT * S], F32R)
    xn_at = place[0]
    xn = sb("xn", [P, TT, D])
    gpost_at = place[0]
    gpost = sb("gpost", [P, D])
    s_at = place[0]
    s_buf = sb("s_buf", [P, 512])
    t_buf = sb("t_buf", [P, 512])
    gpre_at = place[0]
    place[0] += 1536
    pick = sb("pick", [P, TT, P], BF16)
    pickg_at = place[0]
    pickg = sb("pickg", [P, TT, P])
    put_at = place[0]
    put = sb("put", [P, TT, P])
    gpre = sb("gpre", [P, D], at=gpre_at)
    vrows = sb("vrows", [V_ROWS, P], at=gpost_at)
    vec = sb("vec", [P, V_ROWS])
    ident = sb("ident", [P, P])
    iota_row = sb("iota_row", [P, P])
    rw = sb("rw", [P, KT, NE])
    rw_hi = sb("rw_hi", [P, KT * NE], F32R)
    rw_lo = sb("rw_lo", [P, KT * NE], F32R)
    small = sb("small", [P, 64])
    rt = sb("rt", [P, 320])
    ev = sb("ev", [1, 8], I32)
    assert place[0] <= nc.sbuf_usable_end, place[0]
    end = place[0]

    place[0] = mix_base
    hankel = sb("hankel", [P, 8, S])
    mask_a1 = sb("mask_a1", [P, S])
    mask_c1 = sb("mask_c1", [P, S])
    mask_t0 = sb("mask_t0", [P, P])
    chunk_l = sb("chunk_l", [P, P])
    flip = sb("flip", [P, P])
    invw = sb("invw", [P, 2, S])
    pool_w = sb("pool_w_sb", [P, 2, 2, P])
    rg_wa = sb("rg_wa", [P, 2, 2, P])
    rg_wx = sb("rg_wx", [P, 2, 2, P])
    ffn_at = place[0]
    q_a = sb("q_a", [P, 2, S])
    k_a = sb("k_a", [P, S])
    v_a = sb("v_a", [P, TT, P])
    q_c = sb("q_c", [P, 2, S])
    k_c = sb("k_c", [P, 2, S])
    xd = sb("xd", [P, 2, S + 4])
    gd = sb("gd", [P, 2, S])
    pin = sb("pin", [P, 2, S + 16])
    win_at = place[0]
    win_a = sb("win_a", [P, 2, S + 16])
    win_b = sb("win_b", [P, 2, S + 16])
    pd = sb("pd", [P, 2, S], at=win_at)
    xc = sb("xc", [P, 2, S])
    gr = sb("gr", [P, 2, S])
    gi = sb("gi", [P, 2, S])
    th = sb("th", [P, 2, S])
    aa = sb("aa", [P, 2, S])
    late_at = mix_end - 4 * UNIT
    assert place[0] <= late_at, (place[0], late_at)
    v_c = sb("v_c", [P, TT, S], at=late_at)
    probs_t = sb("probs_t", [P, 3, 512], at=late_at + 2048)
    probs = sb("probs", [P, 3, 512], at=xn_at)
    relrow = sb("relrow", [8, RELW], at=gpost_at + 1024)
    sil = sb("sil", [P, 4, S], at=ffn_at)
    hid = sb("hid", [P, 4, S], at=ffn_at + 4096)
    hid_hi = [sb(f"hid_hi{a}", [P, 4, S], F32R, at=ffn_at + 8192 + 4096 * a) for a in range(2)]
    hid_lo = [sb(f"hid_lo{a}", [P, 4, S], F32R, at=ffn_at + 16384 + 4096 * a) for a in range(2)]
    assert ffn_at + 24576 <= mix_end
    xg_hi, xg_lo = h_hi[:, 0:KT * P], h_lo[:, 0:KT * P]
    mh_hi, mh_lo = (h[:, KT * P:KT * P + 512] for h in (h_hi, h_lo))
    xb12 = [sb("xb1", [P, TT, D], BF16, at=gpost_at), sb("xb2", [P, TT, D], BF16, at=s_at)]
    xb3 = [sb("xb3_0", [P, D], BF16, at=hhi_at + 6144), sb("xb3_1", [P, D], BF16, at=hlo_at + 6144)]
    xb = [[part[:, t, :] for t in range(TT)] for part in xb12] + [[part[:, :] for part in xb3]]
    xr = sb("xr", [P, TT, D], at=base + moe_slot(MOE_UNITS - 2 * NRING) * UNIT * 4)
    glast = sb("glast", [P, D], at=base + moe_slot(MOE_UNITS - 2 * NRING + 1) * UNIT * 4)
    y_slots = sb("y_slots", [P, D], at=xn_at)
    sm_buf = sb("sm_buf", [P, 512], at=xn_at + 4096)
    tm_buf = sb("tm_buf", [P, 512], at=xn_at + 6144)
    tri = sb("tri", [P, P], at=pickg_at)
    ones = sb("ones", [P, P], at=put_at)
    logits_t = sb("logits_t", [NE, S], at=gpre_at)
    r_tmp = sb("r_tmp", [P, 120], at=gpre_at + 1024)
    iota_e = rt[:, 288:296]
    desc_e = rt[:, 296:304]

    bank = [nc.alloc_psum_tensor(f"bank{i}", [P, 512], F32) for i in range(8)]
    x_park = nc.dram_tensor("x_park", (P, TT, D), F32, kind="Internal").ap()
    rel_pad = nc.dram_tensor("rel_pad", (8, RELW), F32, kind="Internal").ap()

    names = {}

    def sem(name):
        names[name] = nc.alloc_semaphore(name)
        return names[name]

    slot_in = [sem(f"slot_in{i}") for i in range(2 * NRING)]
    x_in = [sem("x_in0"), sem("x_in1")]
    vrows_in = sem("vrows_in")
    params_in = sem("params_in")
    rel_in = sem("rel_in")
    rel_out = sem("rel_out")
    hankel_in = sem("hankel_in")
    gpost_in = sem("gpost_in")
    park_out = sem("park_out")
    xr_in = sem("xr_in")
    glast_in = sem("glast_in")
    out_done = sem("out_done")
    hi_done = sem("hi_done")
    lo_done = sem("lo_done")
    unit_used = sem("unit_used")
    rw_hi_done = sem("rw_hi_done")
    rw_lo_done = sem("rw_lo_done")
    gpre_in = sem("gpre_in")
    y_ps = sem("y_ps")
    consts = sem("consts")
    pool_step = sem("pool_step")
    act_step = sem("act_step")
    dve_step = sem("dve_step")
    vec_ps = sem("vec_ps")
    vec_done = sem("vec_done")
    lam_abs = sem("lam_abs")
    lam_exp = sem("lam_exp")
    lam_done = sem("lam_done")
    invw_done = sem("invw_done")
    rel_row = sem("rel_row")
    ssq = sem("ssq")
    ms = sem("ms")
    root = sem("root")
    xn_done = sem("xn_done")
    ht_ps = sem("ht_ps")
    ht_hi = sem("ht_hi")
    ht_lo = sem("ht_lo")
    z_out = sem("z_out")
    pads = sem("pads")
    conv_done = sem("conv_done")
    gates_ps = sem("gates_ps")
    gates_done = sem("gates_done")
    decay_done = sem("decay_done")
    m2_done = sem("m2_done")
    mult_done = sem("mult_done")
    pool_ready = sem("pool_ready")
    pool_ps = sem("pool_ps")
    yb_done = sem("yb_done")
    yd_done = sem("yd_done")
    pe_pair = sem("pe_pair")
    sc_ps = {k: sem(f"sc_ps_{k}") for k in "ac"}
    nmax = {k: sem(f"nmax_{k}") for k in "ac"}
    exp_done = {k: sem(f"exp_{k}") for k in "ac"}
    sink_done = sem("sink_done")
    prob_done = {k: sem(f"prob_{k}") for k in "ac"}
    pt_ps = {k: sem(f"pt_ps_{k}") for k in "ac"}
    pt_out = {k: sem(f"pt_out_{k}") for k in "ac"}
    pv_ps = {k: sem(f"pv_ps_{k}") for k in "ac"}
    y_hi = {k: sem(f"y_hi_{k}") for k in "ac"}
    y_lo = {k: sem(f"y_lo_{k}") for k in "ac"}
    post_ssq = sem("post_ssq")
    post_ms = sem("post_ms")
    post_root = sem("post_root")
    x_done = sem("x_done")
    silu_done = sem("silu_done")
    h_done = sem("h_done")
    t_done = sem("t_done")
    hid_hi_done = sem("hid_hi_done")
    hid_lo_done = sem("hid_lo_done")
    logit_ps = sem("logit_ps")
    logit_out = sem("logit_out")
    logit_t = sem("logit_t")
    gate_arg = sem("gate_arg")
    gate_exp = sem("gate_exp")
    taken = sem("taken")
    rank_ps = sem("rank_ps")
    tables = sem("tables")
    acc_zero = sem("acc_zero")
    y_zero = sem("y_zero")
    y_evac = sem("y_evac")
    p_done = sem("p_done")
    pg_done = sem("pg_done")
    xb1_done = sem("xb1_done")
    xr1_done = sem("xr1_done")
    xb2_done = sem("xb2_done")
    xb3_done = sem("xb3_done")
    gather_ps = sem("gather_ps")
    xg_hi_done = sem("xg_hi_done")
    xg_lo_done = sem("xg_lo_done")
    put_ps = sem("put_ps")
    put_done = sem("put_done")
    scatter_ps = sem("scatter_ps")
    acc_added = sem("acc_added")

    def slot_ap(s):
        return ring_a[:, s, :] if s < NRING else ring_b[:, s - NRING, :]

    def unit_src(l, unit, e=None):
        kind, a, b = unit
        if kind == "win":
            return A["w_in"][l, :, 256 * a:256 * a + 256].rearrange("(k p) c -> p k c", p=P)
        if kind == "wout":
            return A["w_out"][l, 256 * a:256 * a + 256, :].rearrange("(k p) c -> p k c", p=P)
        if e is None:
            gate, up, down = A["ffn_w_gate"][0], A["ffn_w_up"][0], A["ffn_w_down"][0]
        else:
            gate, up, down = (A[f"moe_w_{n}"][0, bass.ds(e, 1)].rearrange("o a b -> (o a) b")
                              for n in ("gate", "up", "down"))
        if kind == "down":
            return down[512 * a + 256 * b:512 * a + 256 * b + 256, :].rearrange("(k p) c -> p k c", p=P)
        w = gate if kind == "gate" else up
        return w[512 * b:512 * b + 512, 512 * a:512 * a + 512].rearrange("(k p) c -> p k c", p=P)

    def unit_dst(s, unit):
        cols = {"win": 256, "wout": 1024, "down": 1024}.get(unit[0], 512)
        return slot_ap(s).rearrange("p (k c) -> p k c", c=cols)

    def load_unit(eng, s, l, unit, e=None):
        src, dst = unit_src(l, unit, e), unit_dst(s, unit)
        if unit == ("win", 0, 0):
            src = src.rearrange("p k (g b d) -> p k b g d", g=2, b=2)
            dst = dst.rearrange("p k (b g d) -> p k b g d", g=2, b=2)
            for b in range(2):
                for g in range(2):
                    eng.dma_start(dst[:, :, b, g], src[:, :, b, g]).then_inc(slot_in[s], 16)
        else:
            eng.dma_start(dst, src).then_inc(slot_in[s], 16)

    def ring_lo(s):
        return ring_a_lo[:, s, :] if s < NRING else ring_b_lo[:, s - NRING, :]

    def part(b):
        return b[:, :].rearrange("p (k s) -> p k s", k=4)

    def h_part(h, q):
        return h[:, :].rearrange("p (k s) -> p k s", k=KT)[:, 4 * (q % 2):4 * (q % 2) + 4, P * (q // 2):P * (q // 2) + P]

    def score_at(kind, t, h):
        if t == 0:
            return 0, h * P, h
        pair, n = (h // 2, h % 2) if kind == "a" else (h % 2, h // 2)
        return 1 + pair, n * S, 4 + 2 * pair + n

    ev_range = dict(min_val=0, max_val=NE - 1)

    def load_passes(eng):
        eng.wait_ge(tables, 1)
        return eng.value_load(ev[0:1, 0:1], min_val=NE, max_val=NE + MAX_EXTRA)

    def load_last(eng):
        return eng.value_load(ev[0:1, 4:5], min_val=NE - 1, max_val=NE + MAX_EXTRA - 1)

    block = nc.Block()
    block.__enter__()

    @block.sync
    def _(sp):
        for t in range(TT):
            sp.dma_start(x[:, t, :], A["x"][0, t * P:t * P + P, :]).then_inc(x_in[t], 16)
        sp.dma_start(gpre[:, :], A["norm_mix_pre"][0].partition_broadcast(P)).then_inc(gpre_in, 16)
        for n, (l, unit) in enumerate(STATIC):
            if n == 1:
                rows = 0
                for name, pat in (("pool_scale", "l (k p) -> (l k) p"), ("conv_b", "l (k p) -> (l k) p"),
                                  ("rg_b_a", "l (k p) -> (l k) p"), ("rg_b_x", "l (k p) -> (l k) p"),
                                  ("rg_lambda", "l (k p) -> (l k) p"), ("conv_w", "l j (k p) -> (l j k) p")):
                    src = A[name].rearrange(pat, p=P)
                    sp.dma_start(vrows[rows:rows + src.shape[0], :], src).then_inc(vrows_in, 16)
                    rows += src.shape[0]
                assert rows == V_ROWS
            if n >= NRING:
                sp.wait_ge(unit_used, n - NRING + 1)
            load_unit(sp, n % NRING, l, unit)

        def expert(i, e, first):
            for m, unit in enumerate(FFN_UNITS):
                s = moe_slot(m)
                if first and m < 2 * NRING:
                    if s < NRING:
                        last = max(n for n in range(NSTATIC) if n % NRING == s)
                        sp.wait_ge(unit_used, last + 1)
                    else:
                        sp.wait_ge(sc_ps["c"], 6)
                        sp.wait_ge(pv_ps["a"], 2)
                        sp.wait_ge(pool_ps, 2)
                        sp.wait_ge(yd_done, 2)
                        if s == 2 * NRING - 1:
                            sp.wait_ge(pv_ps["c"], 2)
                else:
                    sp.wait_ge(unit_used, NSTATIC + MOE_UNITS * i + m - 2 * NRING + 1)
                load_unit(sp, s, 1, unit, e)

        expert(0, 0, True)
        with sp.Fori(1, NE) as i:
            expert(i, i, False)
        n_pass = load_passes(sp)
        with sp.If(n_pass > NE):
            with sp.Fori(NE, n_pass) as i:
                e = sp.value_load(ev[0:1, bass.ds(i - (NE - 1), 1)], **ev_range)
                expert(i, e, False)
        for t in range(TT):
            sp.wait_ge(x_done, 14 + 2 * t)
            sp.dma_start(out[0, t * P:t * P + P, :], x[:, t, :]).then_inc(out_done, 16)
        sp.wait_ge(out_done, 32)

    @block.gpsimd
    def _(gp):
        steps = [0]

        def step(ins):
            steps[0] += 1
            ins.then_inc(pool_step, 1)
            gp.wait_ge(pool_step, steps[0])

        def diag(t, value, mult, pattern):
            step(gp.memset(t[:, :], 0.0))
            step(gp.affine_select(out=t[:, :], in_=t[:, :], compare_op=ALU.not_equal, fill=1.0, base=value,
                                  pattern=pattern, channel_multiplier=mult))

        diag(ident, 0, 1, [[-1, P]])
        gp.engine_nop().then_inc(consts, 1)
        gp.dma_start(relrow[:, 0:2 * RELCLIP + 1], A["rel_bias"].rearrange("l h r -> (l h) r")).then_inc(rel_in, 16)
        for dst in (pool_w, rg_wa, rg_wx):
            step(gp.memset(dst[:, :, :, :], 0.0))
        for src, dst in ((A["pool_w"], pool_w), (A["rg_w_a"], rg_wa), (A["rg_w_x"], rg_wx)):
            v = src.rearrange("l (h a) c e -> a c l h e", a=2)
            for a in range(2):
                gp.dma_start(dst[HD * a:HD * a + HD, :, :, HD * a:HD * a + HD], v[a]).then_inc(params_in, 16)
        gp.dma_start(rw[:, :, :], A["router_w"].rearrange("o (k p) e -> p (o k) e", p=P)).then_inc(params_in, 16)
        gp.dma_start(small[:, 0:8], A["attn_sinks"].rearrange("l h -> (l h)").partition_broadcast(P)).then_inc(params_in, 16)
        def padding():
            for t, n in ((xd, 4), (pin, 16), (win_a, 16), (win_b, 16)):
                step(gp.memset(t[:, :, 0:n], 0.0))
            gp.engine_nop().then_inc(pads, 1)

        padding()
        gp.wait_ge(rel_row, 1)
        gp.dma_start(rel_pad, relrow[:, :]).then_inc(rel_out, 16)
        diag(flip, -(P - 1), 1, [[1, P]])
        step(gp.memset(chunk_l[:, :], 0.0))
        for t in (mask_a1, mask_c1, mask_t0):
            step(gp.memset(t[:, :], 0.0))
        for r in (0, 64):
            step(gp.memset(chunk_l[r:r + 1, 0:64], 1.0))
            step(gp.memset(chunk_l[r + 32:r + 33, 64:128], 1.0))
            step(gp.memset(mask_t0[r:r + 1, 64:128], NEG))
            step(gp.memset(mask_a1[r:r + 1, 0:64], NEG))
            step(gp.memset(mask_a1[r:r + 1, 192:256], NEG))
            step(gp.memset(mask_a1[r + 32:r + 33, 0:128], NEG))
            step(gp.memset(mask_c1[r:r + 1, 192:256], NEG))
        step(gp.iota(iota_row[:, :], pattern=[[1, P]], base=0, channel_multiplier=0,
                     allow_small_or_imprecise_dtypes=True))
        step(gp.iota(iota_e, pattern=[[1, NE]], base=0, channel_multiplier=0, allow_small_or_imprecise_dtypes=True))
        step(gp.iota(desc_e, pattern=[[-1, NE]], base=NE, channel_multiplier=0, allow_small_or_imprecise_dtypes=True))
        step(gp.iota(invw[:, :, :], pattern=[[0, 2], [1, S]], base=1, channel_multiplier=0,
                     allow_small_or_imprecise_dtypes=True))
        gp.engine_nop().then_inc(consts, 1)
        gp.wait_ge(rel_out, 16)
        gp.dma_start(hankel[:, :, :], bass.AP(rel_pad.tensor, 1, [[1, P], [RELW, 8], [1, S]])).then_inc(hankel_in, 16)

        W = S + 16
        for l in range(2):
            if l == 1:
                gp.wait_ge(x_done, 8)
                gp.wait_ge(pool_ps, 1)
                padding()
            gp.wait_ge(z_out, 8 * l + 3)
            step(gp.tensor_tensor(win_a[:, :, 1:W], pin[:, :, 1:W], pin[:, :, 0:W - 1], ALU.add))
            step(gp.tensor_tensor(win_b[:, :, 2:W], win_a[:, :, 2:W], win_a[:, :, 0:W - 2], ALU.add))
            step(gp.tensor_copy(win_b[0:64, 0, :], win_a[0:64, 0, :]))
            step(gp.tensor_tensor(win_a[:, 1, 4:W], win_b[:, 1, 4:W], win_b[:, 1, 0:W - 4], ALU.add))
            step(gp.tensor_copy(win_b[0:64, 1, :], win_a[0:64, 1, :]))
            step(gp.tensor_tensor(win_b[64:P, 1, 8:W], win_a[64:P, 1, 8:W], win_a[64:P, 1, 0:W - 8], ALU.add))
            if l == 0:
                gp.wait_ge(invw_done, 1)
            step(gp.tensor_tensor(pd[:, :, :], win_b[:, :, 16:W], invw[:, :, :], ALU.mult))
            gp.tensor_tensor(pd[:, :, :], pd[:, :, :], pin[:, :, 16:W], ALU.subtract).then_inc(pool_ready, 1)
        gp.wait_ge(xn_done, 16)
        step(gp.memset(ones[:, :], 1.0))
        step(gp.memset(tri[:, :], 1.0))
        gp.affine_select(out=tri[:, :], in_=tri[:, :], compare_op=ALU.is_gt, fill=0.0, base=0,
                         pattern=[[1, P]], channel_multiplier=-1).then_inc(consts, 1)
        gp.wait_ge(logit_ps, 1)
        for t in range(TT):
            gp.wait_ge(xb2_done, t + 1)
            gp.tensor_tensor(xb[2][t], xn[:, t, :], xb[1][t], ALU.subtract).then_inc(xb3_done, 1)
        gp.wait_ge(rank_ps, 1)
        gp.memset(put[:, :, :], 0.0).then_inc(put_done, 1)
        gp.wait_ge(park_out, 16)
        gp.memset(x[:, :, :], 0.0).then_inc(acc_zero, 1)

    @block.scalar
    def _(act):
        next_hi = [0]

        def hi(u, slot=None, uses=None, buf=None):
            slot = u % NRING if slot is None else slot
            buf = u % NHI if buf is None else buf
            act.wait_ge(slot_in[slot], 16 * (loads(u, slot) if uses is None else uses))
            if not isinstance(u, int) or u >= NHI:
                act.wait_ge(unit_used, u - NHI + 1)
            nc.scalar.activation(w_hi[:, buf, :], slot_ap(slot), ACT.Copy).then_inc(hi_done, 1)

        def hi_to(u):
            for n in range(next_hi[0], min(u + 1, NSTATIC)):
                hi(n)
            next_hi[0] = max(next_hi[0], u + 1)

        warmed = [0]

        def warm(func):
            warmed[0] += 1
            nc.scalar.activation(rt[:, 312 + warmed[0]:313 + warmed[0]], rt[:, 312:313], func)

        def post_square(n, q, src, junk, ready):
            ready(q)
            if q > 1:
                act.wait_ge(post_ssq, 4 * n + q - 1)
            nc.scalar.activation(junk(q), src(q), ACT.Square, accum_out=small[:, 12 + q:13 + q]).then_inc(post_ssq, 1)

        def post_rooted(n, t):
            act.wait_ge(post_ms, 2 * n + t + 1)
            nc.scalar.activation(small[:, 16 + t:17 + t], small[:, 16 + t:17 + t], ACT.Sqrt, scale=1.0 / D)\
                .then_inc(post_root, 1)

        def pre_square(n, q):
            t = q // 2
            sl = slice(512 * (q % 2), 512 * (q % 2) + 512)
            if n == 0:
                act.wait_ge(x_in[t], 16)
            else:
                act.wait_ge(x_done, 4 * (n - 1) + q + 1)
            nc.scalar.activation(xn[:, t, sl], x[:, t, sl], ACT.Square, accum_out=small[:, 8 + q:9 + q]).then_inc(ssq, 1)

        def pre_rooted(n, t):
            act.wait_ge(ms, 2 * n + t + 1)
            nc.scalar.activation(small[:, 18 + t:19 + t], small[:, 18 + t:19 + t], ACT.Sqrt, scale=1.0 / D)\
                .then_inc(root, 1)

        def h_evac(n, q):
            act.wait_ge(ht_ps, 4 * n + q + 1)
            nc.scalar.activation(h_part(h_hi, q), part(bank[4 + q]), ACT.Copy).then_inc(ht_hi, 1)

        def z_evac(l, q):
            act.wait_ge(unit_used, LAYER_AT[l] + q + 1)
            b = bank[q % 2]
            v = b[:, :].rearrange("p (a s) -> p a s", a=2)
            if q == 0:
                r = nc.scalar.activation(xd[:, :, 4:S + 4], v, ACT.Copy)
            elif q == 1:
                r = nc.scalar.activation(gd[:, :, :], v, ACT.Gelu_apprx_tanh)
            elif q == 2:
                if l == 1:
                    act.wait_ge(pool_ready, 1)
                r = nc.scalar.activation(pin[:, :, 16:S + 16], v, ACT.Copy)
            elif q == 3:
                r = nc.scalar.activation(q_a[:, :, :], v, ACT.Copy, scale=HD ** -0.5)
            elif q == 4:
                nc.scalar.activation(k_a[:, :], b[:, 0:S], ACT.Copy)
                r = nc.scalar.activation(v_a[:, :, :].rearrange("p a s -> p (a s)"), b[:, S:2 * S], ACT.Copy)
            elif q == 5:
                r = nc.scalar.activation(q_c[:, :, :], v, ACT.Copy, scale=HD ** -0.5)
            elif q == 6:
                r = nc.scalar.activation(k_c[:, :, :], v, ACT.Copy)
            else:
                r = nc.scalar.activation(v_c[:, :, :], v, ACT.Copy)
            r.then_inc(z_out, 1)

        def exps(l, kind):
            bk = [bank[5], bank[6], bank[7]] if kind == "a" else [bank[0], bank[1], bank[3]]
            act.wait_ge(nmax[kind], l + 1)
            if kind == "c":
                act.wait_ge(pt_ps["a"], 3 * l + 3)
            o = 20 if kind == "a" else 36
            for t in range(TT):
                for h in range(4):
                    w = P * (t + 1)
                    b, c, n = score_at(kind, t, h)
                    r = nc.scalar.activation(probs[:, b, c:c + w], bk[b][:, c:c + w], ACT.Exp,
                                             bias=small[:, o + n:o + n + 1], accum_out=small[:, o + 8 + n:o + 9 + n])
            r.then_inc(exp_done[kind], 1)
            if kind == "a":
                act.wait_ge(sink_done, l + 1)
                nc.scalar.activation(small[:, 52:60], small[:, 52:60], ACT.Exp).then_inc(exp_done[kind], 1)

        def pt_evac(l, kind):
            bk = [bank[5], bank[6], bank[7]] if kind == "a" else [bank[0], bank[1], bank[3]]
            if kind == "c":
                act.wait_ge(pv_ps["a"], l + 1)
            for b in range(3):
                act.wait_ge(pt_ps[kind], 3 * l + b + 1)
                nc.scalar.activation(probs_t[:, b, :], bk[b][:, :], ACT.Copy).then_inc(pt_out[kind], 1)

        def y_evac_hi(l, kind):
            act.wait_ge(pv_ps[kind], l + 1)
            act.wait_ge(unit_used, LAYER_AT[l] + 8)
            k = 0 if kind == "a" else 4
            nc.scalar.activation(h_hi[:, k * S:(k + 2) * S], bank[2][:, :], ACT.Copy).then_inc(y_hi[kind], 1)

        posts = [A["norm_mix_post"][0], A["norm_ffn_post"][0], A["norm_mix_post"][1]]
        pres = [A["norm_mix_pre"][0], A["norm_ffn_pre"][0], A["norm_mix_pre"][1], A["norm_ffn_pre"][1]]

        def junk(q):
            return xn[:, q // 2, 512 * (q % 2):512 * (q % 2) + 512]

        def next_pre(n):
            act.wait_ge(xn_done, 4 * n)
            act.dma_start(gpre[:, :], pres[n].partition_broadcast(P)).then_inc(gpre_in, 16)

        def next_post(n):
            if n:
                act.wait_ge(x_done, 4 * n)
            act.dma_start(gpost[:, :], posts[n].partition_broadcast(P)).then_inc(gpost_in, 16)

        def block_end(last, n):
            def ready(q):
                if q < 3:
                    act.wait_ge(y_ps, 3 * n + q + 1)
                else:
                    act.wait_ge(unit_used, last + 1)
            warm(ACT.Sqrt)
            def y(q):
                return bank[4 + q][:, :]
            post_square(n, 0, y, junk, ready)
            post_square(n, 1, y, junk, ready)
            post_rooted(n, 0)
            pre_square(n + 1, 0)
            pre_square(n + 1, 1)
            post_square(n, 2, y, junk, ready)
            pre_rooted(n + 1, 0)
            post_square(n, 3, y, junk, ready)
            post_rooted(n, 1)
            h_evac(n + 1, 0)
            h_evac(n + 1, 1)
            pre_square(n + 1, 2)
            pre_square(n + 1, 3)
            pre_rooted(n + 1, 1)
            h_evac(n + 1, 2)
            h_evac(n + 1, 3)

        for q in range(4):
            pre_square(0, q)
            if q % 2:
                pre_rooted(0, q // 2)
        for q in range(4):
            h_evac(0, q)
        for l in range(2):
            u0 = LAYER_AT[l]
            if l == 1:
                next_post(2)
                next_pre(3)
            for q in range(6):
                hi_to(u0 + q + (LEAD if l == 1 or q > 2 else 2 + q))
                z_evac(l, q)
                if l == 0 and q == 1:
                    act.wait_ge(lam_abs, 1)
                    nc.scalar.activation(small[:, 60:64], small[:, 60:64], ACT.Exp, scale=-1.0).then_inc(lam_exp, 1)
                    act.wait_ge(rel_out, 16)
                    next_post(0)
                    next_pre(1)
                if l == 0 and q == 3:
                    act.wait_ge(params_in, 16 * 8)
                    nc.scalar.activation(rw_hi[:, :], rw[:, :, :].rearrange("p k e -> p (k e)"), ACT.Copy)\
                        .then_inc(rw_hi_done, 1)
                if q == 4:
                    act.wait_ge(gates_ps, l + 1)
                    for dst, b, c in ((gr, 2, V_BA), (gi, 3, V_BX)):
                        for t in range(2):
                            r = nc.scalar.activation(dst[:, t, :], bank[b][:, t * S:t * S + S], ACT.Sigmoid,
                                                     bias=vec[:, c + 2 * l + t:c + 2 * l + t + 1])
                            if dst is gr and t == 1:
                                r.then_inc(act_step, 1)
                    r.then_inc(gates_done, 1)
                    act.wait_ge(act_step, l + 1)
                    act.wait_ge(lam_done, 1)
                    for t in range(2):
                        nc.scalar.activation(th[:, t, :], gr[:, t, :], ACT.Tanh,
                                             scale=rt[:, 304 + 2 * l + t:305 + 2 * l + t])
                    for t in range(2):
                        r = nc.scalar.activation(aa[:, t, :], gr[:, t, :], ACT.Exp,
                                                 scale=rt[:, 308 + 2 * l + t:309 + 2 * l + t])
                    r.then_inc(decay_done, 1)
            hi_to(u0 + 5 + LEAD)
            exps(l, "a")
            z_evac(l, 6)
            act.wait_ge(m2_done, l + 1)
            nc.scalar.activation(th[:, :, :], th[:, :, :], ACT.Sqrt).then_inc(mult_done, 1)
            z_evac(l, 7)
            hi_to(u0 + 6 + LEAD)
            pt_evac(l, "a")
            y_evac_hi(l, "a")
            exps(l, "c")
            hi_to(u0 + 8 + LEAD)
            pt_evac(l, "c")
            hi_to(u0 + 9 + LEAD)
            y_evac_hi(l, "c")
            hi_to(u0 + 10 + LEAD)
            block_end(u0 + 11, 2 * l)
            if l == 1:
                break
            next_post(1)
            next_pre(2)
            f0 = FFN0_AT
            hi_to(f0 + LEAD)
            for j in range(FB):
                at = FFN_AT["gate", j, 1]
                hi_to(f0 + at + LEAD)
                act.wait_ge(unit_used, f0 + at + 1)
                if j > 0:
                    act.wait_ge(h_done, j)
                nc.scalar.activation(sil[:, 0:2, :].rearrange("p a s -> p (a s)"), bank[0][:, :], ACT.Silu)
                nc.scalar.activation(sil[:, 2:4, :].rearrange("p a s -> p (a s)"), bank[1][:, :], ACT.Silu)\
                    .then_inc(silu_done, 1)
                hi_to(f0 + FFN_AT["up", j, 1] + LEAD)
                act.wait_ge(h_done, j + 1)
                if j > 1:
                    act.wait_ge(unit_used, f0 + FFN_AT["down", j - 2, 1] + 1)
                nc.scalar.activation(hid_hi[j % 2][:, :, :], hid[:, :, :], ACT.Copy).then_inc(hid_hi_done, 1)
            hi_to(f0 + MOE_UNITS - 2 + LEAD)
            block_end(f0 + MOE_UNITS - 1, 1)

        act.dma_start(x_park, x[:, :, :]).then_inc(park_out, 16)
        for t in range(TT):
            act.wait_ge(xn_done, 14 + 2 * t)
            nc.scalar.activation(xb[0][t], xn[:, t, :], ACT.Copy).then_inc(xb1_done, 1)
        for t in range(TT):
            act.wait_ge(xr1_done, t + 1)
            nc.scalar.activation(xb[1][t], xn[:, t, :], ACT.Copy).then_inc(xb2_done, 1)
        warm(ACT.Exp)

        def hi_moe(i, m):
            s = moe_slot(m)
            before = loads(NSTATIC - 1, s) if s < NRING else 0
            per = MOE_UNITS // (2 * NRING)
            hi(NSTATIC + MOE_UNITS * i + m, slot=s, uses=before + per * i + m // (2 * NRING) + 1,
               buf=(NSTATIC + m) % NHI)

        def xg_evac(i):
            for b in range(2):
                act.wait_ge(gather_ps, 2 * i + b + 1)
                nc.scalar.activation(xg_hi[:, 512 * b:512 * b + 512], bank[5 + b][:, :], ACT.Copy).then_inc(xg_hi_done, 1)

        def mh_evac(i, j):
            act.wait_ge(t_done, FB * i + j + 1)
            nc.scalar.activation(mh_hi, bank[4][:, :], ACT.Copy).then_inc(hid_hi_done, 1)

        def one_pass(i, last):
            m = LEAD
            for j in range(FB):
                at = FFN_AT["gate", j, 1]
                for m in range(m, min(at + LEAD, MOE_UNITS - 1) + 1):
                    hi_moe(i, m)
                m += 1
                act.wait_ge(unit_used, NSTATIC + MOE_UNITS * i + at + 1)
                act.wait_ge(h_done, FB * (i + 1) + j)
                nc.scalar.activation(sm_buf[:, :], bank[0][:, :], ACT.Silu).then_inc(silu_done, 1)
                if j > 0:
                    mh_evac(i, j - 1)
            for m in range(m, MOE_UNITS):
                hi_moe(i, m)
            if last:
                free = NSTATIC + MOE_UNITS * i + MOE_UNITS - 2 * NRING
                act.wait_ge(unit_used, free + 2)
                act.dma_start(xr[:, :, :], x_park).then_inc(xr_in, 16)
                act.dma_start(glast[:, :], A["norm_ffn_post"][1].partition_broadcast(P)).then_inc(glast_in, 16)
            if last:
                mh_evac(i, FB - 1)
            else:
                hi_moe(i + 1, 0)
                hi_moe(i + 1, 1)
                mh_evac(i, FB - 1)
                xg_evac(i + 1)
                for m in range(2, LEAD):
                    hi_moe(i + 1, m)

        hi_moe(0, 0)
        act.wait_ge(gate_arg, 1)
        nc.scalar.activation(rt[:, 64:66], rt[:, 64:66], ACT.Exp).then_inc(gate_exp, 1)
        warm(ACT.Silu)
        hi_moe(0, 1)
        xg_evac(0)
        for m in range(2, LEAD):
            hi_moe(0, m)
        n_pass = load_passes(act)
        last_pass = load_last(act)
        with act.Fori(0, last_pass) as i:
            one_pass(i, False)
        one_pass(last_pass, True)
        warm(ACT.Sqrt)
        for q in range(4):
            post_square(3, q, lambda q: x[:, q // 2, 512 * (q % 2):512 * (q % 2) + 512],
                        lambda q: xg_hi[:, 512 * (q % 2):512 * (q % 2) + 512],
                        lambda q: act.wait_ge(acc_added, 4 * n_pass + q + 1))
            if q % 2:
                post_rooted(3, q // 2)

    @block.vector
    def _(dve):
        steps = [0]

        def step(ins):
            steps[0] += 1
            ins.then_inc(dve_step, 1)
            dve.wait_ge(dve_step, steps[0])

        V = nc.vector

        next_lo = [0]

        def lo(u, slot=None, buf=None):
            slot = u % NRING if slot is None else slot
            buf = u % NHI if buf is None else buf
            dve.wait_ge(hi_done, u + 1)
            V.tensor_tensor(ring_lo(slot), slot_ap(slot), w_hi[:, buf, :], ALU.subtract).then_inc(lo_done, 1)

        def lo_to(u):
            for n in range(next_lo[0], min(u + 1, NSTATIC)):
                lo(n)
            next_lo[0] = max(next_lo[0], u + 1)

        eps_sum = rt[:, 312:313]
        t_bufs = (t_buf, s_buf)

        def h_low(n, q):
            dve.wait_ge(ht_hi, 4 * n + q + 1)
            V.tensor_tensor(h_part(h_lo, q), part(bank[4 + q]), h_part(h_hi, q), ALU.subtract).then_inc(ht_lo, 1)

        def block_norms(n, scale, res, pre):
            def mean_sum(t, at, dst, sem_in, count, sem_out):
                dve.wait_ge(sem_in, count)
                a = at + 2 * t
                V.scalar_tensor_tensor(small[:, dst + t:dst + t + 1], small[:, a:a + 1], small[:, a + 1:a + 2],
                                       eps_sum, ALU.add, ALU.add).then_inc(sem_out, 1)

            def post_sum(t):
                mean_sum(t, 12, 16, post_ssq, 4 * n + 2 * t + 2, post_ms)

            def pre_sum(t):
                mean_sum(t, 8, 18, ssq, 4 * pre + 2 * t + 2, ms)

            def inverse(t, at, sem_in, count):
                dve.wait_ge(sem_in, count)
                step(V.reciprocal(small[:, at + t:at + t + 1], small[:, at + t:at + t + 1]))

            def update(q):
                t, c = q // 2, slice(512 * (q % 2), 512 * (q % 2) + 512)
                y = bank[4 + q][:, :] if n < 3 else x[:, t, c]
                b = t_bufs[q % 2] if n < 3 else (tm_buf, sm_buf)[q % 2]
                if q > 1:
                    dve.wait_ge(x_done, 4 * n + q - 1)
                step(V.scalar_tensor_tensor(b[:, :], y, small[:, 16 + t:17 + t], scale(q), ALU.mult, ALU.mult))
                V.tensor_tensor(x[:, t, c], res[:, t, c], b[:, :], ALU.add).then_inc(x_done, 1)

            def apply(q):
                t, c = q // 2, slice(512 * (q % 2), 512 * (q % 2) + 512)
                V.scalar_tensor_tensor(xn[:, t, c], x[:, t, c], small[:, 18 + t:19 + t], gpre[:, c], ALU.mult, ALU.mult)\
                    .then_inc(xn_done, 1)

            def post(t):
                inverse(t, 16, post_root, 2 * n + t + 1)
                update(2 * t)
                update(2 * t + 1)

            def pre_scale(t):
                pre_sum(t)
                inverse(t, 18, root, 2 * pre + t + 1)
                dve.wait_ge(gpre_in, 16 * (pre + 1))
                if n is not None:
                    dve.wait_ge(x_done, 4 * n + 2 * t + 2)

            if n is None:
                for t in range(TT):
                    pre_scale(t)
                    apply(2 * t)
                    apply(2 * t + 1)
                for q in range(4):
                    h_low(pre, q)
            elif pre is None:
                for t in range(TT):
                    post_sum(t)
                    post(t)
            else:
                post_sum(0)
                post(0)
                pre_scale(0)
                apply(0)
                post_sum(1)
                apply(1)
                post(1)
                h_low(pre, 0)
                h_low(pre, 1)
                pre_scale(1)
                apply(2)
                apply(3)
                h_low(pre, 2)
                h_low(pre, 3)

        def nmaxes(l, kind):
            bk = [bank[5], bank[6], bank[7]] if kind == "a" else [bank[0], bank[1], bank[3]]
            o = 20 if kind == "a" else 36
            for b in range(3):
                dve.wait_ge(sc_ps[kind], 3 * l + b + 1)
                n = 4 if b == 0 else 2
                at = o + (0 if b == 0 else 2 + 2 * b)
                r = V.tensor_reduce(small[:, at:at + n], bk[b][:, :].rearrange("p (h k) -> p h k", h=n), AX.X, ALU.max,
                                    negate=True)
            if kind == "c":
                r.then_inc(nmax[kind], 1)
                return
            step(r)
            sink = small[:, 4 * l:4 * l + 4]
            for t in range(TT):
                m = small[:, o + 4 * t:o + 4 * t + 4]
                r = V.scalar_tensor_tensor(m, sink, -1.0, m, ALU.mult, ALU.min)
            r.then_inc(nmax[kind], 1)
            dve.wait_ge(nmax[kind], l + 1)
            for t in range(TT):
                r = V.tensor_tensor(small[:, 52 + 4 * t:56 + 4 * t], sink, small[:, o + 4 * t:o + 4 * t + 4], ALU.add)
            r.then_inc(sink_done, 1)

        def normalise(l, kind):
            o = 20 if kind == "a" else 36
            dve.wait_ge(exp_done[kind], 2 * l + 2 if kind == "a" else l + 1)
            total = small[:, o + 8:o + 16]
            if kind == "a":
                step(V.tensor_tensor(total, total, small[:, 52:60], ALU.add))
            step(V.reciprocal(total, total))
            for t in range(TT):
                for h in range(4):
                    w = P * (t + 1)
                    b, c, n = score_at(kind, t, h)
                    r = V.tensor_scalar(probs[:, b, c:c + w], probs[:, b, c:c + w], small[:, o + 8 + n:o + 9 + n], None,
                                        ALU.mult)
            r.then_inc(prob_done[kind], 1)

        def y_evac_lo(l, kind):
            dve.wait_ge(y_hi[kind], l + 1)
            k = 0 if kind == "a" else 4
            V.tensor_tensor(h_lo[:, k * S:(k + 2) * S], bank[2][:, :], h_hi[:, k * S:(k + 2) * S], ALU.subtract)\
                .then_inc(y_lo[kind], 1)

        step(V.memset(eps_sum, D * EPS))
        block_norms(None, None, None, 0)
        dve.wait_ge(rel_in, 16)
        V.tensor_copy(relrow[:, 2 * RELCLIP + 1:RELW],
                      relrow[:, 2 * RELCLIP:2 * RELCLIP + 1].to_broadcast([8, RELW - 2 * RELCLIP - 1])).then_inc(rel_row, 1)

        def decay_scales():
            lam = vec[:, V_LAM:V_LAM + 4]
            y, z, z2, p = (rt[:, 4 * a:4 * a + 4] for a in range(4))
            step(V.tensor_scalar(y, lam, -1.0, None, ALU.mult))
            V.tensor_tensor(small[:, 60:64], lam, y, ALU.max).then_inc(lam_abs, 1)
            dve.wait_ge(lam_exp, 1)
            step(V.tensor_scalar(z, small[:, 60:64], 2.0, None, ALU.add))
            step(V.reciprocal(z, z))
            step(V.tensor_tensor(z, z, small[:, 60:64], ALU.mult))
            step(V.tensor_tensor(z2, z, z, ALU.mult))
            step(V.tensor_scalar(p, z2, 1.0 / 17, None, ALU.mult))
            for n in (15, 13, 11, 9, 7, 5, 3):
                step(V.scalar_tensor_tensor(p, p, 1.0 / n, z2, ALU.add, ALU.mult))
            step(V.scalar_tensor_tensor(p, p, 1.0, z, ALU.add, ALU.mult))
            step(V.tensor_scalar(y, y, 0.0, None, ALU.max))
            step(V.scalar_tensor_tensor(p, p, 2.0, y, ALU.mult, ALU.add))
            V.tensor_scalar(rt[:, 304:308], p, 8.0, None, ALU.mult)
            V.tensor_scalar(rt[:, 308:312], p, -8.0, None, ALU.mult).then_inc(lam_done, 1)


        for l in range(2):
            u0 = LAYER_AT[l]
            if l == 0:
                lo_to(2)
                dve.wait_ge(vec_ps, 1)
                V.tensor_copy(vec[:, :], bank[2][:, 0:V_ROWS]).then_inc(vec_done, 1)
                dve.wait_ge(vec_done, 1)
            else:
                lo_to(u0 + LEAD)
            dve.wait_ge(z_out, 8 * l + 1)
            dve.wait_ge(pads, l + 1)
            for j in (3, 2, 1, 0):
                for t in range(2):
                    c = V_CONVW + (l * 4 + j) * 2 + t
                    src = xd[:, t, j + 1:j + 1 + S]
                    if j == 3:
                        b = V_CONVB + 2 * l + t
                        r = V.tensor_scalar(xc[:, t, :], src, vec[:, c:c + 1], vec[:, b:b + 1], ALU.mult, ALU.add)
                    else:
                        r = V.scalar_tensor_tensor(xc[:, t, :], src, vec[:, c:c + 1], xc[:, t, :], ALU.mult, ALU.add)
                if j:
                    step(r)
            r.then_inc(conv_done, 1)
            if l == 0:
                lo_to(3)
                decay_scales()
            lo_to(u0 + 3 + LEAD)
            if l == 0:
                dve.wait_ge(rw_hi_done, 1)
                V.tensor_tensor(rw_lo[:, :], rw[:, :, :].rearrange("p k e -> p (k e)"), rw_hi[:, :], ALU.subtract)\
                    .then_inc(rw_lo_done, 1)
                dve.wait_ge(consts, 2)
                for t, c, w in ((0, 0, 2.0), (0, 64, 4.0), (1, 0, 8.0), (1, 64, 16.0)):
                    r = V.tensor_scalar(invw[c:c + 64, t, :], invw[c:c + 64, t, :], w, None, ALU.min)
                step(r)
                V.reciprocal(invw[:, :, :], invw[:, :, :]).then_inc(invw_done, 1)
            lo_to(u0 + 4 + LEAD)
            dve.wait_ge(decay_done, l + 1)
            V.tensor_tensor(gi[:, :, :], gi[:, :, :], xc[:, :, :], ALU.mult)
            step(V.tensor_tensor(gr[:, :, :], aa[:, :, :], aa[:, :, :], ALU.mult))
            V.scalar_tensor_tensor(th[:, :, :], gr[:, :, :], 1.0, th[:, :, :], ALU.add, ALU.mult).then_inc(m2_done, 1)
            lo_to(u0 + 5 + LEAD)
            nmaxes(l, "a")
            normalise(l, "a")
            dve.wait_ge(mult_done, l + 1)
            step(V.tensor_tensor(gi[:, :, :], gi[:, :, :], th[:, :, :], ALU.mult))
            for t in range(2):
                r = V.tensor_tensor_scan(gr[:, t, :], aa[:, t, :], gi[:, t, :], 0.0, ALU.mult, ALU.add)
            step(r)
            step(V.tensor_tensor(gd[:, :, :], gd[:, :, :], gr[:, :, :], ALU.mult))
            lo_to(u0 + 6 + LEAD)
            dve.wait_ge(pool_ps, l + 1)
            dve.wait_ge(unit_used, u0 + 8)
            for t in range(2):
                sl = slice((2 + t) * S, (3 + t) * S)
                c = V_PSCALE + 2 * l + t
                step(V.tensor_scalar(h_hi[:, sl], bank[4][:, t * S:t * S + S], vec[:, c:c + 1], None, ALU.mult))
                r = V.scalar_tensor_tensor(h_lo[:, sl], bank[4][:, t * S:t * S + S], vec[:, c:c + 1], h_hi[:, sl],
                                           ALU.mult, ALU.subtract)
            r.then_inc(yb_done, 1)
            sl = slice(6 * S, 8 * S)
            gdf = gd[:, :, :].rearrange("p a s -> p (a s)")
            step(V.tensor_copy(h_hi[:, sl], gdf))
            V.tensor_tensor(h_lo[:, sl], gdf, h_hi[:, sl], ALU.subtract).then_inc(yd_done, 1)
            nmaxes(l, "c")
            y_evac_lo(l, "a")
            normalise(l, "c")
            lo_to(u0 + 9 + LEAD)
            y_evac_lo(l, "c")
            lo_to(u0 + 10 + LEAD)
            dve.wait_ge(gpost_in, 16 * (2 * l + 1))

            def gpost_part(q):
                return gpost[:, 512 * (q % 2):512 * (q % 2) + 512]

            block_norms(2 * l, gpost_part, x, 2 * l + 1)
            if l == 1:
                break
            f0 = FFN0_AT
            lo_to(f0 + LEAD)
            for j in range(FB):
                at = FFN_AT["up", j, 1]
                lo_to(f0 + at + LEAD - 1)
                dve.wait_ge(silu_done, j + 1)
                dve.wait_ge(unit_used, f0 + at + 1)
                if j > 0:
                    dve.wait_ge(hid_lo_done, j)
                for a in range(2):
                    r = V.tensor_tensor(hid[:, 2 * a:2 * a + 2, :].rearrange("p a s -> p (a s)"),
                                        sil[:, 2 * a:2 * a + 2, :].rearrange("p a s -> p (a s)"),
                                        bank[2 + a][:, :], ALU.mult)
                r.then_inc(h_done, 1)
                lo_to(f0 + at + LEAD)
                dve.wait_ge(hid_hi_done, j + 1)
                V.tensor_tensor(hid_lo[j % 2][:, :, :], hid[:, :, :], hid_hi[j % 2][:, :, :], ALU.subtract).then_inc(hid_lo_done, 1)
            lo_to(f0 + MOE_UNITS - 2 + LEAD)
            dve.wait_ge(gpost_in, 32)
            block_norms(1, gpost_part, x, 2)

        def lo_moe(i, m):
            lo(NSTATIC + MOE_UNITS * i + m, slot=moe_slot(m), buf=(NSTATIC + m) % NHI)

        def r3(at):
            return rt[:, at:at + 16].rearrange("p (t e) -> p t e", t=TT)

        def bc(ap):
            return ap.unsqueeze(2).to_broadcast([P, TT, NE])

        def bce(ap):
            return ap.unsqueeze(1).to_broadcast([P, TT, NE])

        lg, eq, oh1, oh2, g, sel = (r3(16 * a) for a in range(5 + 1))
        stab = rt[:, 96:120].rearrange("p (t c) -> p t c", t=TT)
        gtab = rt[:, 120:144].rearrange("p (t c) -> p t c", t=TT)
        m1, mx, m2, den = (rt[:, 144 + 2 * a:146 + 2 * a] for a in range(4))
        cnt, over, order = rt[:, 152:160], rt[:, 160:168], rt[:, 168:176]
        selx = rt[:, 176:200].rearrange("p (i e) -> p i e", i=MAX_EXTRA)
        tabs = rt[:, 96:144].rearrange("p (b c) -> p b c", b=2 * TT)
        tmp4 = r_tmp[:, 0:96].rearrange("p (b i e) -> p b i e", b=2 * TT, i=MAX_EXTRA)
        tmpx = r_tmp[:, 96:120].rearrange("p (i e) -> p i e", i=MAX_EXTRA)
        lst = rt[:, 224:229]
        arg = rt[:, 64:66]

        for t in range(TT):
            dve.wait_ge(xb1_done, t + 1)
            V.tensor_tensor(xn[:, t, :], xn[:, t, :], xb[0][t], ALU.subtract).then_inc(xr1_done, 1)
        dve.wait_ge(logit_ps, 1)
        V.tensor_copy(logits_t[:, :], bank[0][0:NE, 0:S]).then_inc(logit_out, 1)
        dve.wait_ge(logit_t, 1)
        step(V.tensor_copy(lg, bank[1][:, 0:TT * NE].rearrange("p (t e) -> p t e", t=TT)))

        def one_hot(dst, src, top):
            step(V.tensor_reduce(top, src, AX.X, ALU.max))
            step(V.tensor_tensor(eq, src, bc(top), ALU.is_equal))
            step(V.tensor_tensor(sel, eq, bce(desc_e), ALU.mult))
            step(V.tensor_reduce(mx, sel, AX.X, ALU.max))
            step(V.tensor_tensor(dst, sel, bc(mx), ALU.is_equal))

        one_hot(oh1, lg, m1)
        step(V.scalar_tensor_tensor(lg, oh1, -3.0e38, lg, ALU.mult, ALU.add))
        one_hot(oh2, lg, m2)
        V.tensor_tensor(sel, oh1, oh2, ALU.add).then_inc(taken, 1)
        V.tensor_tensor(arg, m2, m1, ALU.subtract).then_inc(gate_arg, 1)
        V.memset(stab, NO_SLOT)
        V.memset(gtab, 0.0)
        dve.wait_ge(taken, 1)
        step(V.tensor_scalar(eq, sel, -NO_SLOT, NO_SLOT, ALU.mult, ALU.add))
        dve.wait_ge(rank_ps, 1)
        step(V.tensor_tensor(stab[:, :, 0:NE], eq, bank[1][:, 0:TT * NE].rearrange("p (t e) -> p t e", t=TT), ALU.add))
        for t in range(TT):
            r = V.tensor_scalar(pick[:, t, :], iota_row[:, :], stab[:, t, 0:1], None, ALU.is_equal)
        r.then_inc(p_done, 1)
        step(V.tensor_copy(cnt, bank[1][:, TT * NE:(TT + 1) * NE]))
        step(V.tensor_scalar(over, cnt, float(P), None, ALU.is_gt))
        step(V.memset(cnt, 1.0))
        V.tensor_tensor_scan(order, cnt, over, 0.0, ALU.mult, ALU.add)
        dve.wait_ge(gate_exp, 1)
        step(V.tensor_scalar(den, arg, 1.0, None, ALU.add))
        step(V.reciprocal(den, den))
        for i in range(MAX_EXTRA):
            V.scalar_tensor_tensor(selx[:, i, :], order, float(i + 1), over, ALU.is_equal, ALU.mult)
        V.tensor_tensor(mx, arg, den, ALU.mult)
        V.tensor_scalar(lst[:, 4:5], order[:, NE - 1:NE], float(NE - 1), None, ALU.add)
        step(V.tensor_scalar(lst[:, 0:1], order[:, NE - 1:NE], float(NE), None, ALU.add))
        V.tensor_tensor(tmpx, selx, iota_e.unsqueeze(1).to_broadcast([P, MAX_EXTRA, NE]), ALU.mult)
        V.tensor_tensor(oh1, oh1, bc(den), ALU.mult)
        step(V.tensor_tensor(oh2, oh2, bc(mx), ALU.mult))
        V.tensor_tensor(gtab[:, :, 0:NE], oh1, oh2, ALU.add)
        step(V.tensor_reduce(lst[:, 1:1 + MAX_EXTRA], tmpx, AX.X, ALU.add))
        V.tensor_copy(ev[0:1, 0:5], lst[0:1, :]).then_inc(tables, 1)
        lo_moe(0, 0)
        step(V.tensor_tensor(tmp4, selx.unsqueeze(1).to_broadcast([P, 2 * TT, MAX_EXTRA, NE]),
                             tabs[:, :, 0:NE].unsqueeze(2).to_broadcast([P, 2 * TT, MAX_EXTRA, NE]), ALU.mult))
        step(V.tensor_reduce(tabs[:, :, NE:NE + MAX_EXTRA], tmp4, AX.X, ALU.add))
        V.tensor_scalar(stab[:, :, NE:NE + MAX_EXTRA], stab[:, :, NE:NE + MAX_EXTRA], -float(P), None, ALU.add)

        def picks(i):
            for t in range(TT):
                r = V.tensor_scalar(pick[:, t, :], iota_row[:, :], stab[:, t, bass.ds(i, 1)], None, ALU.is_equal)
            r.then_inc(p_done, 1)

        def xg_lows(i):
            for b in range(2):
                dve.wait_ge(xg_hi_done, 2 * i + b + 1)
                V.tensor_tensor(xg_lo[:, 512 * b:512 * b + 512], bank[5 + b][:, :], xg_hi[:, 512 * b:512 * b + 512],
                                ALU.subtract).then_inc(xg_lo_done, 1)

        def y_out(i):
            dve.wait_ge(unit_used, NSTATIC + MOE_UNITS * i)
            for a in range(2):
                r = V.tensor_copy(y_slots[:, 512 * a:512 * a + 512], bank[2 + a][:, :])
            r.then_inc(y_evac, 1)

        def add_scatter(i):
            for q in range(4):
                dve.wait_ge(scatter_ps, 4 * i + q + 1)
                sl = x[:, q // 2, 512 * (q % 2):512 * (q % 2) + 512]
                V.tensor_tensor(sl, sl, bank[[5, 6, 7, 4][q]][:, :], ALU.add).then_inc(acc_added, 1)

        def mh_low(i, j):
            dve.wait_ge(hid_hi_done, FB * (i + 1) + j + 1)
            V.tensor_tensor(mh_lo, bank[4][:, :], mh_hi, ALU.subtract).then_inc(hid_lo_done, 1)

        def one_pass(i, last):
            m = LEAD
            y_out(i)
            for j in range(FB):
                at = FFN_AT["up", j, 1]
                for m in range(m, min(at + LEAD - 1, MOE_UNITS - 1) + 1):
                    lo_moe(i, m)
                    if j > 0 and m == FFN_AT["gate", j, 1] + LEAD:
                        mh_low(i, j - 1)
                m += 1
                dve.wait_ge(silu_done, FB * (i + 1) + j + 1)
                dve.wait_ge(unit_used, NSTATIC + MOE_UNITS * i + at + 1)
                if j > 0:
                    dve.wait_ge(t_done, FB * i + j)
                V.tensor_tensor(tm_buf[:, :], sm_buf[:, :], bank[1][:, :], ALU.mult).then_inc(h_done, 1)
                if j == 0:
                    add_scatter(i)
                    dve.wait_ge(gather_ps, 2 * i + 2)
                    picks(i + 1)
                    for t in range(TT):
                        r = V.tensor_scalar(pickg[:, t, :], iota_row[:, :], stab[:, t, bass.ds(i, 1)],
                                            gtab[:, t, bass.ds(i, 1)], ALU.is_equal, ALU.mult)
                    r.then_inc(pg_done, 1)
                if j == 4:
                    dve.wait_ge(put_ps, i + 1)
                    V.tensor_copy(put[:, :, :].rearrange("p t s -> p (t s)"), bank[7][:, 0:TT * P]).then_inc(put_done, 1)
            if last:
                mh_low(i, FB - 1)
            else:
                lo_moe(i + 1, 0)
                lo_moe(i + 1, 1)
                mh_low(i, FB - 1)
                xg_lows(i + 1)
                for m in range(2, LEAD):
                    lo_moe(i + 1, m)

        lo_moe(0, 1)
        xg_lows(0)
        for m in range(2, LEAD):
            lo_moe(0, m)
        dve.wait_ge(acc_zero, 1)
        dve.wait_ge(y_zero, 1)
        dve.wait_ge(xb3_done, 2)
        n_pass = load_passes(dve)
        last_pass = load_last(dve)
        with dve.Fori(0, last_pass) as i:
            one_pass(i, False)
        one_pass(last_pass, True)
        y_out(n_pass)
        add_scatter(n_pass)
        dve.wait_ge(xr_in, 16)
        dve.wait_ge(glast_in, 16)
        block_norms(3, lambda q: glast[:, 512 * (q % 2):512 * (q % 2) + 512], xr, None)

    @block.tensor
    def _(pe):
        T = nc.tensor

        def split_mm(dst, l_hi, l_lo, r_hi, r_lo, first, last):
            T.matmul(dst, l_lo, r_hi, start=first, stop=False, skip_group_check=True)
            T.matmul(dst, l_hi, r_lo, start=False, stop=False, skip_group_check=True)
            return T.matmul(dst, l_hi, r_hi, start=False, stop=last, skip_group_check=True)

        pairs = [0]

        def ht(k, c, n):
            return slice(k * S + c, k * S + c + n)

        def keep_warm(n):
            for _ in range(n):
                T.matmul(bank[3][:, 0:P], ident[:, :], ident[:, :], start=True, stop=True)

        def transpose_h(n):
            for q in range(4):
                if q == 2 and n > 0:
                    keep_warm(12)
                t, k0 = q // 2, 4 * (q % 2)
                pe.wait_ge(xn_done, 4 * n + q + 1)
                for k in range(4):
                    r = T.transpose(bank[4 + q][:, k * P:k * P + P], xn[:, t, (k0 + k) * P:(k0 + k) * P + P], ident[:, :])
                r.then_inc(ht_ps, 1)

        def h_wait(n, k):
            pe.wait_ge(ht_lo, 4 * n + 3 + k // 4)

        def block_quarter(r, q):
            if q < 3:
                r.then_inc(y_ps, 1)

        def w_in(l, q):
            u = LAYER_AT[l] + q
            c = WIN_ORDER[q]
            buf = u % NHI
            wh = w_hi[:, buf, :].rearrange("p (k c) -> p k c", c=256)
            wl = ring_lo(u % NRING).rearrange("p (k c) -> p k c", c=256)
            pe.wait_ge(lo_done, u + 1)
            if q >= 2:
                pe.wait_ge(z_out, 8 * l + q - 1)
            dst = bank[q % 2]
            for a in range(2):
                if c == 5 or (c == 1 and a == 1):
                    continue
                for k in range(KT):
                    if q == 0 and a == 0 and k % 4 == 0:
                        h_wait(2 * l, k)
                    lh, ll = wh[:, k, a * P:a * P + P], wl[:, k, a * P:a * P + P]
                    r = split_mm(dst[:, a * S:a * S + S], lh, ll, h_hi[:, ht(k, 0, S)], h_lo[:, ht(k, 0, S)],
                                 k == 0, k == KT - 1)
            if c in (1, 5):
                n, c0 = (P, P) if c == 1 else (S, 0)
                o = S if c == 1 else 0
                for t in range(TT):
                    for k in range(KT):
                        r = split_mm(dst[:, o + t * n:o + t * n + n], h_hi[:, ht(k, t * P, P)], h_lo[:, ht(k, t * P, P)],
                                     wh[:, k, c0:c0 + n], wl[:, k, c0:c0 + n], k == 0, k == KT - 1)
            r.then_inc(unit_used, 1)

        def blocks(dst, w, l, src):
            for n in range(2):
                r = T.matmul(dst[:, n * S:n * S + S], w[:, l, n, :], src[:, n, :], start=True, stop=True)
            return r

        def scores(l, kind):
            bk = [bank[5], bank[6], bank[7]] if kind == "a" else [bank[0], bank[1], bank[3]]
            for t in range(TT):
                m, ranges = ((mask_t0, [(64, 128)]) if t == 0 else
                             (mask_a1, [(0, 128), (192, 256)]) if kind == "a" else (mask_c1, [(192, 256)]))
                for pair in range(2):
                    rows = slice(HD * pair, HD * pair + HD)
                    for n in range(2):
                        h = 2 * pair + n if kind == "a" else 2 * n + pair
                        w = P * (t + 1)
                        b, c, _ = score_at(kind, t, h)
                        dst = bk[b][:, c:c + w]
                        q, k = (q_a[rows, n, :], k_a[rows, :]) if kind == "a" else (q_c[rows, n, :], k_c[rows, n, :])
                        T.matmul(dst, q[:, t * P:t * P + P], k[:, 0:w], start=True, stop=False, skip_group_check=True)
                        for a, z in ranges:
                            r = T.matmul(bk[b][:, c + a:c + z], chunk_l[rows, :], m[rows, a:z], start=False,
                                         stop=(kind == "a"), skip_group_check=True)
                        for kt in range(t + 1 if kind == "c" else 0):
                            j = P * (t - kt)
                            r = T.matmul(bk[b][:, c + kt * P:c + kt * P + P], hankel[:, 4 * l + h, j:j + P], flip[:, :],
                                         start=False, stop=True, skip_group_check=True)
                    if t == 0 and pair == 0:
                        r.then_inc(pe_pair, 1)
                        pairs[0] += 1
                        pe.wait_ge(pe_pair, pairs[0])
                    else:
                        r.then_inc(sc_ps[kind], 1)

        def transposes(l, kind):
            bk = [bank[5], bank[6], bank[7]] if kind == "a" else [bank[0], bank[1], bank[3]]
            pe.wait_ge(prob_done[kind], l + 1)
            for g in range(3):
                for h in range(4):
                    b, c, _ = score_at(kind, min(g, 1), h)
                    c += P * (g == 2)
                    r = T.transpose(bk[g][:, h * P:h * P + P], probs[:, b, c:c + P], ident[:, :])
                r.then_inc(pt_ps[kind], 1)

        def values(l, kind):
            pe.wait_ge(pt_out[kind], 3 * l + 3)
            if kind == "c":
                pe.wait_ge(y_lo["a"], l + 1)
            for h in range(4):
                rows = slice(HD * (h % 2), HD * (h % 2) + HD)
                for t in range(TT):
                    for kt in range(t + 1):
                        v = v_a[:, kt, HD * (h // 2):HD * (h // 2) + HD] if kind == "a" else v_c[:, kt, HD * h:HD * h + HD]
                        r = T.matmul(bank[2][rows, (h // 2) * S + t * P:(h // 2) * S + t * P + P], v,
                                     probs_t[:, t + kt, h * P:h * P + P], start=(kt == 0), stop=(kt == t))
            r.then_inc(pv_ps[kind], 1)

        def w_out(l, n, t):
            u = LAYER_AT[l] + 8 + n
            k0 = 2 * WOUT_ORDER[n]
            buf = u % NHI
            pe.wait_ge(lo_done, u + 1)
            pe.wait_ge([yb_done, yd_done, y_lo["a"], y_lo["c"]][n], l + 1)
            for a in range(2):
                for k in range(2):
                    c = k * D + 512 * a
                    r = split_mm(bank[4 + 2 * t + a][:, :], h_hi[:, ht(k0 + k, t * P, P)], h_lo[:, ht(k0 + k, t * P, P)],
                                 w_hi[:, buf, c:c + 512], ring_lo(u % NRING)[:, c:c + 512],
                                 n == 0 and k == 0, n == 3 and k == 1)
                if n == 3:
                    block_quarter(r, 2 * t + a)
            if t == 1:
                r.then_inc(unit_used, 1)

        pe.wait_ge(consts, 1)
        keep_warm(12)
        transpose_h(0)
        keep_warm(12)
        for l in range(2):
            for q in range(4):
                w_in(l, q)
                if l == 0 and q == 0:
                    pe.wait_ge(vrows_in, 16 * 6)
                    T.transpose(bank[2][:, 0:V_ROWS], vrows[:, :], ident[0:V_ROWS, 0:V_ROWS]).then_inc(vec_ps, 1)
            pe.wait_ge(conv_done, l + 1)
            pe.wait_ge(params_in, 16 * 8)
            blocks(bank[2], rg_wa, l, xc)
            blocks(bank[3], rg_wx, l, xc).then_inc(gates_ps, 1)
            w_in(l, 4)
            w_in(l, 5)
            pe.wait_ge(consts, 2)
            pe.wait_ge(z_out, 8 * l + 5)
            scores(l, "a")
            pe.wait_ge(pool_ready, l + 1)
            blocks(bank[4], pool_w, l, pd).then_inc(pool_ps, 1)
            w_in(l, 6)
            w_in(l, 7)
            transposes(l, "a")
            pe.wait_ge(hankel_in, 16)
            pe.wait_ge(z_out, 8 * l + 8)
            pe.wait_ge(gates_done, l + 1)
            scores(l, "c")
            values(l, "a")
            for n, t in ((0, 0), (0, 1), (1, 0)):
                w_out(l, n, t)
            transposes(l, "c")
            w_out(l, 1, 1)
            values(l, "c")
            for n, t in ((2, 0), (3, 0), (2, 1), (3, 1)):
                w_out(l, n, t)
            transpose_h(2 * l + 1)
            if l == 1:
                break
            f0 = FFN0_AT
            for j in range(FB + 1):
                if j < FB:
                    for kind, b0, free in (("gate", 0, silu_done), ("up", 2, h_done)):
                        for b in range(2):
                            u = f0 + FFN_AT[kind, j, b]
                            buf = u % NHI
                            pe.wait_ge(lo_done, u + 1)
                            if j > 0 and b == 0:
                                pe.wait_ge(free, j)
                            for f in range(4):
                                if j == 0 and kind == "gate" and f == 0:
                                    h_wait(1, 4 * b)
                                for k in range(4):
                                    c = k * 512 + f * P
                                    kk = 4 * b + k
                                    r = split_mm(bank[b0 + f // 2][:, (f % 2) * S:(f % 2) * S + S],
                                                 w_hi[:, buf, c:c + P], ring_lo(u % NRING)[:, c:c + P],
                                                 h_hi[:, ht(kk, 0, S)], h_lo[:, ht(kk, 0, S)],
                                                 kk == 0 and f % 2 == 0, kk == KT - 1)
                            r.then_inc(unit_used, 1)
                if j > 0:
                    pe.wait_ge(hid_lo_done, j)
                    order = [(0, 0), (0, 1), (1, 0), (1, 1)] if j < FB else [(0, 0), (1, 0), (0, 1), (1, 1)]
                    for b, t in order:
                        u = f0 + FFN_AT["down", j - 1, b]
                        buf = u % NHI
                        pe.wait_ge(lo_done, u + 1)
                        for a in range(2):
                            for f in range(2):
                                c = f * D + 512 * a
                                ff = 2 * b + f
                                r = split_mm(bank[4 + 2 * t + a][:, :], hid_hi[(j - 1) % 2][:, ff, t * P:t * P + P],
                                             hid_lo[(j - 1) % 2][:, ff, t * P:t * P + P], w_hi[:, buf, c:c + 512],
                                             ring_lo(u % NRING)[:, c:c + 512], j == 1 and ff == 0,
                                             j == FB and ff == 3)
                            if j == FB and b == 1:
                                block_quarter(r, 2 * t + a)
                        if t == 1:
                            r.then_inc(unit_used, 1)
            transpose_h(2)

        pe.wait_ge(rw_lo_done, 1)
        for k in range(KT):
            if k % 4 == 0:
                h_wait(3, k)
            r = split_mm(bank[0][0:NE, 0:S], rw_hi[:, k * NE:k * NE + NE], rw_lo[:, k * NE:k * NE + NE],
                         h_hi[:, ht(k, 0, S)], h_lo[:, ht(k, 0, S)], k == 0, k == KT - 1)
        r.then_inc(logit_ps, 1)
        pe.wait_ge(logit_out, 1)
        for t in range(TT):
            r = T.transpose(bank[1][:, t * NE:t * NE + NE], logits_t[:, t * P:t * P + P], ident[0:NE, 0:NE])
        r.then_inc(logit_t, 1)
        keep_warm(9)
        pe.wait_ge(consts, 3)
        pe.wait_ge(taken, 1)
        m = rt[:, 80:96].rearrange("p (t e) -> p t e", t=TT)
        T.matmul(bank[1][:, 0:NE], tri[:, :], m[:, 0, :], start=True, stop=True)
        T.matmul(bank[1][:, NE:2 * NE], ones[:, :], m[:, 0, :], start=True, stop=False)
        T.matmul(bank[1][:, NE:2 * NE], tri[:, :], m[:, 1, :], start=False, stop=True)
        T.matmul(bank[1][:, 2 * NE:3 * NE], ones[:, :], m[:, 0, :], start=True, stop=False)
        T.matmul(bank[1][:, 2 * NE:3 * NE], ones[:, :], m[:, 1, :], start=False, stop=True).then_inc(rank_ps, 1)

        def gather():
            for b in range(2):
                for a in range(4):
                    k = 4 * b + a
                    for part in range(3):
                        for t in range(TT):
                            r = T.matmul(bank[5 + b][:, a * P:a * P + P], xb[part][t][:, k * P:k * P + P], pick[:, t, :],
                                         start=(part == 0 and t == 0), stop=(part == 2 and t == TT - 1))
                r.then_inc(gather_ps, 1)

        def scatter(i):
            pe.wait_ge(y_evac, i + 1)
            pe.wait_ge(put_done, i + 1)
            for q in range(4):
                if q == 3:
                    pe.wait_ge(hid_lo_done, FB * (i + 1))
                T.matmul(bank[[5, 6, 7, 4][q]][:, :], put[:, q // 2, :], y_slots[:, 512 * (q % 2):512 * (q % 2) + 512],
                         start=True, stop=True).then_inc(scatter_ps, 1)

        def unit_wait(i, unit):
            m = FFN_AT[unit]
            pe.wait_ge(lo_done, NSTATIC + MOE_UNITS * i + m + 1)
            return (NSTATIC + m) % NHI, ring_lo(moe_slot(m))

        def up_proj(i, j, kind, dst, free):
            for b in range(2):
                buf, w_lo = unit_wait(i, (kind, j, b))
                if b == 0:
                    pe.wait_ge(free, FB * (i + 1) + j)
                for k in range(4):
                    kk = 4 * b + k
                    r = split_mm(dst[:, :], xg_hi[:, kk * P:kk * P + P], xg_lo[:, kk * P:kk * P + P],
                                 w_hi[:, buf, k * 512:k * 512 + 512], w_lo[:, k * 512:k * 512 + 512],
                                 kk == 0, kk == KT - 1)
                r.then_inc(unit_used, 1)

        def turn(i, j):
            pe.wait_ge(h_done, FB * (i + 1) + j + 1)
            pe.wait_ge(hid_lo_done, FB * (i + 1) + j)
            if j == 0:
                pe.wait_ge(acc_added, 4 * i + 4)
            for f in range(4):
                r = T.transpose(bank[4][:, f * P:f * P + P], tm_buf[:, f * P:f * P + P], ident[:, :])
            r.then_inc(t_done, 1)

        def down_proj(i, j):
            pe.wait_ge(hid_lo_done, FB * (i + 1) + j + 1)
            if j == 0:
                pe.wait_ge(y_evac, i + 1)
            for b in range(2):
                buf, w_lo = unit_wait(i, ("down", j, b))
                for f in range(2):
                    ff = 2 * b + f
                    for a in range(2):
                        c = f * D + 512 * a
                        r = split_mm(bank[2 + a][:, :], mh_hi[:, ff * P:ff * P + P], mh_lo[:, ff * P:ff * P + P],
                                     w_hi[:, buf, c:c + 512], w_lo[:, c:c + 512],
                                     j == 0 and ff == 0, j == FB - 1 and ff == 3)
                r.then_inc(unit_used, 1)
            return r

        pe.wait_ge(p_done, 1)
        pe.wait_ge(xb3_done, 2)
        gather()
        pe.wait_ge(put_done, 1)
        for a in range(2):
            for half in range(2):
                r = T.matmul(bank[2 + a][:, half * TT * P:half * TT * P + TT * P], put[:, 0, :],
                             put[:, :, :].rearrange("p t s -> p (t s)"), start=True, stop=True)
        r.then_inc(y_zero, 1)
        n_pass = load_passes(pe)
        def one_pass(i, last):
            pe.wait_ge(xg_lo_done, 2 * i + 2)
            for j in range(FB):
                up_proj(i, j, "gate", bank[0], silu_done)
                if j > 0:
                    turn(i, j - 1)
                up_proj(i, j, "up", bank[1], h_done)
                if j == 0:
                    scatter(i)
                if j == 3:
                    pe.wait_ge(pg_done, i + 1)
                    for t in range(TT):
                        r = T.transpose(bank[7][:, t * P:t * P + P], pickg[:, t, :], ident[:, :])
                    r.then_inc(put_ps, 1)
                if j > 0:
                    down_proj(i, j - 1)
            turn(i, FB - 1)
            if not last:
                pe.wait_ge(p_done, i + 2)
                gather()
            down_proj(i, FB - 1)

        last_pass = load_last(pe)
        with pe.Fori(0, last_pass) as i:
            one_pass(i, False)
        one_pass(last_pass, True)
        scatter(n_pass)

    block.__exit__(None, None, None)


_INS = ["x", "norm_mix_pre", "w_in", "attn_sinks", "pool_w", "pool_scale", "rel_bias", "conv_w", "conv_b",
        "rg_w_a", "rg_b_a", "rg_w_x", "rg_b_x", "rg_lambda", "w_out", "norm_mix_post", "norm_ffn_pre",
        "norm_ffn_post", "ffn_w_gate", "ffn_w_up", "ffn_w_down", "router_w", "moe_w_gate", "moe_w_up", "moe_w_down"]


def kernel(**inputs):
    import numpy as np
    import concourse.bacc as bacc
    from concourse.bass_utils import run_bass_kernel_spmd

    nc = bacc.Bacc("TRN2", target_bir_lowering=False, num_devices=1)
    arrays, args = {}, {}
    for name in _INS:
        a = np.ascontiguousarray(inputs[name])
        arrays[f"in_{name}"] = a
        args[name] = nc.dram_tensor(f"in_{name}", a.shape, mybir.dt.from_np(a.dtype), kind="ExternalInput").ap()
    out = nc.dram_tensor("out_x", (1, S, D), F32, kind="ExternalOutput").ap()
    build(nc, args, out)
    return run_bass_kernel_spmd(nc, [arrays], core_ids=[0]).results[0]["out_x"]
```
